# Optimizing a Trainium2 kernel written in Bass

```python
import jax, jax.numpy as jnp
from jax import lax
import numpy as np

D_MODEL = 1024
BATCH = 1
SEQ = 512
DEPTH = 1
DEC_BATCH = 8
DEC_SEQ = 1
PAST_LEN = 4096
PAGE_SIZE = 128

HEAD_SIZE = 64
N_HEADS = D_MODEL // HEAD_SIZE
D_RWKV = N_HEADS * HEAD_SIZE
D_DECAY_LORA = 64
D_AAA_LORA = 64
D_GATE_LORA = 128
POOL_WINDOWS = (2, 4, 8, 16)
N_POOL_GROUPS = len(POOL_WINDOWS)
POOL_GROUP = D_MODEL // 8
D_POOL = N_POOL_GROUPS * POOL_GROUP
POOL_BUF = max(POOL_WINDOWS) - 1
D_FF = (D_MODEL * 11) // 4
CONV_W = 3
D_SHIFT = 3 * D_RWKV + D_DECAY_LORA + D_AAA_LORA + D_GATE_LORA
IN_COLS = D_SHIFT + D_POOL + 2 * D_MODEL
ALPHA = float((2 * DEPTH) ** 0.25)
BETA = float((8 * DEPTH) ** -0.25)
LN_EPS = 1e-5
GN_EPS = 64e-5

kernel_name = 'hybrid_pool_rwkv7_convffn_deepnorm_step'

def layer_norm(x, w=None, b=None):
    xf = x.astype(jnp.float32)
    mu = jnp.mean(xf, axis=-1, keepdims=True)
    var = jnp.mean(jnp.square(xf - mu), axis=-1, keepdims=True)
    y = (xf - mu) * lax.rsqrt(var + LN_EPS)
    if w is not None:
        y = y * w + b
    return y

def rwkv7_recurrence(state0, r, w, k, v, kk, a):
    def step(S, inp):
        r_t, w_t, k_t, v_t, kk_t, a_t = inp
        sa = jnp.einsum('bhvk,bhk->bhv', S, kk_t)
        S = (S * w_t[:, :, None, :]
             - sa[..., None] * (kk_t * a_t)[:, :, None, :]
             + v_t[..., None] * k_t[:, :, None, :])
        y = jnp.einsum('bhvk,bhk->bhv', S, r_t)
        return S, y
    xs = (jnp.moveaxis(r, 1, 0), jnp.moveaxis(w, 1, 0), jnp.moveaxis(k, 1, 0),
          jnp.moveaxis(v, 1, 0), jnp.moveaxis(kk, 1, 0), jnp.moveaxis(a, 1, 0))
    S, ys = lax.scan(step, state0, xs)
    return jnp.moveaxis(ys, 0, 1), S

def pool_mix(p_in, buf, pos0, pool_w, pool_scale):
    B, T, _ = p_in.shape
    ext = jnp.concatenate([buf.astype(jnp.float32), p_in.astype(jnp.float32)], axis=1)
    cs = jnp.pad(jnp.cumsum(ext, axis=1), ((0, 0), (1, 0), (0, 0)))
    end = cs[:, POOL_BUF + 1:]
    pos = pos0 + jnp.arange(T)
    groups = []
    for g, win in enumerate(POOL_WINDOWS):
        sl = slice(g * POOL_GROUP, (g + 1) * POOL_GROUP)
        start = cs[:, POOL_BUF + 1 - win: POOL_BUF + 1 - win + T, sl]
        cnt = jnp.minimum(win, pos + 1).astype(jnp.float32)[None, :, None]
        groups.append((end[..., sl] - start) / cnt)
    pooled = jnp.stack(groups, axis=2)
    diff = pooled - p_in.astype(jnp.float32).reshape(B, T, N_POOL_GROUPS, POOL_GROUP)
    mixed = jnp.einsum('btgc,gcd->btgd', diff, pool_w).reshape(B, T, D_POOL) * pool_scale
    return mixed, ext[:, -POOL_BUF:]

def token_mixer(h, shift_prev, wkv_prev, pool_prev, pos0, l, p):
    B, T, _ = h.shape
    w_in = p['w_in'][l]
    proj = jnp.einsum('btd,de->bte', h, w_in)
    prev_proj = jnp.einsum('bd,de->be', shift_prev.astype(jnp.float32), w_in[:, :D_SHIFT])
    cur = proj[..., :D_SHIFT]
    prev_rows = jnp.concatenate([prev_proj[:, None], cur[:, :-1]], axis=1)
    xs = cur + (prev_rows - cur) * p['mu_shift'][l]
    splits = [D_RWKV, 2 * D_RWKV, 3 * D_RWKV, 3 * D_RWKV + D_DECAY_LORA,
              3 * D_RWKV + D_DECAY_LORA + D_AAA_LORA]
    r, k, v, wl, al, gl = jnp.split(xs, splits, axis=-1)
    w_log = -jax.nn.softplus(-(p['decay_w0'][l] + jnp.tanh(wl) @ p['decay_up'][l])) - 0.5
    decay = jnp.exp(-jnp.exp(w_log))
    a = jax.nn.sigmoid(p['aaa_a0'][l] + al @ p['aaa_up'][l])
    g = jax.nn.sigmoid(gl) @ p['gate_up'][l]
    kk = k * p['k_k'][l]
    k = k * (1.0 + (a - 1.0) * p['k_a'][l])
    hs = lambda t: t.reshape(B, T, N_HEADS, HEAD_SIZE)
    kk_h = hs(kk)
    kk_h = kk_h / jnp.maximum(jnp.sqrt(jnp.sum(jnp.square(kk_h), axis=-1, keepdims=True)), 1e-12)
    r_h, k_h, v_h = hs(r), hs(k), hs(v)
    y, S_new = rwkv7_recurrence(wkv_prev.astype(jnp.float32), r_h, hs(decay), k_h, v_h, kk_h, hs(a))
    mu = jnp.mean(y, axis=-1, keepdims=True)
    var = jnp.mean(jnp.square(y - mu), axis=-1, keepdims=True)
    y = ((y - mu) * lax.rsqrt(var + GN_EPS)).reshape(B, T, D_RWKV) * p['gn_w'][l] + p['gn_b'][l]
    bonus = jnp.sum(r_h * k_h * p['r_k'][l], axis=-1, keepdims=True) * v_h
    y = y + bonus.reshape(B, T, D_RWKV)
    y_rwkv = (y * g) @ p['w_branch_rwkv'][l]
    p_in = proj[..., D_SHIFT:D_SHIFT + D_POOL]
    pooled, pool_new = pool_mix(p_in, pool_prev, pos0, p['pool_w'][l], p['pool_scale'][l])
    y_pool = pooled @ p['w_branch_pool'][l]
    gate_pool, gate_rwkv = jnp.split(proj[..., D_SHIFT + D_POOL:], 2, axis=-1)
    merged = jax.nn.sigmoid(gate_pool) * y_pool + jax.nn.sigmoid(gate_rwkv) * y_rwkv
    out = merged @ p['w_out'][l]
    return out, h[:, -1], S_new, pool_new

def conv_ffn(h, conv_prev, l, p):
    T = h.shape[1]
    u = jnp.einsum('btd,df->btf', h, p['ffn_up'][l])
    ext = jnp.concatenate([conv_prev.astype(jnp.float32), u], axis=1)
    cw = p['conv_w'][l]
    conv = p['conv_b'][l] + ext[:, 0:T] * cw[0] + ext[:, 1:T + 1] * cw[1] + ext[:, 2:T + 2] * cw[2]
    val, gate = jnp.split(conv, 2, axis=-1)
    out = (val * jax.nn.silu(gate)) @ p['ffn_down'][l]
    return out, ext[:, -(CONV_W - 1):]

def run_trunk(x, c, pos0, shift_st, wkv_st, pool_st, conv_st, p):
    x = x.astype(jnp.float32)
    c = c.astype(jnp.float32)
    n_shift, n_wkv, n_pool, n_conv = [], [], [], []
    for l in range(DEPTH):
        mod = jnp.einsum('bd,de->be', c, p['ada_w'][l]) + p['ada_b'][l]
        sh1, sc1, g1, sh2, sc2, g2 = jnp.split(mod[:, None, :], 6, axis=-1)
        h = layer_norm(x) * (1.0 + sc1) + sh1
        mix, s_shift, s_wkv, s_pool = token_mixer(h, shift_st[l], wkv_st[l], pool_st[l], pos0, l, p)
        x = layer_norm(ALPHA * x + (1.0 + g1) * mix, p['ln1_w'][l], p['ln1_b'][l])
        h2 = layer_norm(x) * (1.0 + sc2) + sh2
        ff, s_conv = conv_ffn(h2, conv_st[l], l, p)
        x = layer_norm(ALPHA * x + (1.0 + g2) * ff, p['ln2_w'][l], p['ln2_b'][l])
        n_shift.append(s_shift)
        n_wkv.append(s_wkv)
        n_pool.append(s_pool)
        n_conv.append(s_conv)
    return x, jnp.stack(n_shift), jnp.stack(n_wkv), jnp.stack(n_pool), jnp.stack(n_conv)

def setup_inputs(seed: int = 0) -> dict:
    key = jax.random.key(seed)
    ks = iter(jax.random.split(key, 48))
    nrm = lambda shape, s: jax.random.normal(next(ks), shape, jnp.float32) * s
    L, D = DEPTH, D_MODEL
    return {
        'x_prompt': nrm((BATCH, SEQ, D), 1.0),
        'x_sample': nrm((DEC_BATCH, DEC_SEQ, D), 1.0),
        'state_shift': nrm((L, DEC_BATCH, D), 1.0),
        'state_wkv': nrm((L, DEC_BATCH, N_HEADS, HEAD_SIZE, HEAD_SIZE), 0.3),
        'state_pool': nrm((L, DEC_BATCH, POOL_BUF, D_POOL), 1.0),
        'state_conv': nrm((L, DEC_BATCH, CONV_W - 1, 2 * D_FF), 1.0),
        'c_prompt': nrm((BATCH, D), 1.0),
        'c_sample': nrm((DEC_BATCH, D), 1.0),
        'ada_w': nrm((L, D, 6 * D), 0.2 * D ** -0.5),
        'ada_b': nrm((L, 6 * D), 0.02),
        'w_in': nrm((L, D, IN_COLS), D ** -0.5),
        'mu_shift': jax.random.uniform(next(ks), (L, D_SHIFT), jnp.float32),
        'decay_w0': jnp.linspace(-6.0, 1.0, D_RWKV, dtype=jnp.float32)[None, :] + nrm((L, D_RWKV), 0.1),
        'decay_up': nrm((L, D_DECAY_LORA, D_RWKV), 0.1 * D_DECAY_LORA ** -0.5),
        'aaa_a0': nrm((L, D_RWKV), 0.1),
        'aaa_up': nrm((L, D_AAA_LORA, D_RWKV), 0.5 * D_AAA_LORA ** -0.5),
        'gate_up': nrm((L, D_GATE_LORA, D_RWKV), D_GATE_LORA ** -0.5),
        'k_k': 0.85 + nrm((L, D_RWKV), 0.05),
        'k_a': 1.0 + nrm((L, D_RWKV), 0.05),
        'r_k': nrm((L, N_HEADS, HEAD_SIZE), 0.1),
        'gn_w': 1.0 + nrm((L, D_RWKV), 0.05),
        'gn_b': nrm((L, D_RWKV), 0.01),
        'w_branch_rwkv': nrm((L, D_RWKV, D), D_RWKV ** -0.5),
        'pool_w': nrm((L, N_POOL_GROUPS, POOL_GROUP, POOL_GROUP), POOL_GROUP ** -0.5),
        'pool_scale': 1.0 + nrm((L, D_POOL), 0.05),
        'w_branch_pool': nrm((L, D_POOL, D), D_POOL ** -0.5),
        'w_out': nrm((L, D, D), BETA * D ** -0.5),
        'ln1_w': 1.0 + nrm((L, D), 0.05),
        'ln1_b': nrm((L, D), 0.01),
        'ffn_up': nrm((L, D, 2 * D_FF), D ** -0.5),
        'conv_w': nrm((L, CONV_W, 2 * D_FF), CONV_W ** -0.5),
        'conv_b': nrm((L, 2 * D_FF), 0.01),
        'ffn_down': nrm((L, D_FF, D), BETA * D_FF ** -0.5),
        'ln2_w': 1.0 + nrm((L, D), 0.05),
        'ln2_b': nrm((L, D), 0.01),
    }

def reference(x_prompt, x_sample, state_shift, state_wkv, state_pool, state_conv, c_prompt, c_sample,
              ada_w, ada_b, w_in, mu_shift, decay_w0, decay_up, aaa_a0, aaa_up, gate_up, k_k, k_a, r_k,
              gn_w, gn_b, w_branch_rwkv, pool_w, pool_scale, w_branch_pool, w_out, ln1_w, ln1_b,
              ffn_up, conv_w, conv_b, ffn_down, ln2_w, ln2_b):
    p = {'ada_w': ada_w, 'ada_b': ada_b, 'w_in': w_in, 'mu_shift': mu_shift, 'decay_w0': decay_w0,
         'decay_up': decay_up, 'aaa_a0': aaa_a0, 'aaa_up': aaa_up, 'gate_up': gate_up, 'k_k': k_k,
         'k_a': k_a, 'r_k': r_k, 'gn_w': gn_w, 'gn_b': gn_b, 'w_branch_rwkv': w_branch_rwkv,
         'pool_w': pool_w, 'pool_scale': pool_scale, 'w_branch_pool': w_branch_pool, 'w_out': w_out,
         'ln1_w': ln1_w, 'ln1_b': ln1_b, 'ffn_up': ffn_up, 'conv_w': conv_w, 'conv_b': conv_b,
         'ffn_down': ffn_down, 'ln2_w': ln2_w, 'ln2_b': ln2_b}
    B = x_prompt.shape[0]
    f32 = jnp.float32
    z_shift = jnp.zeros((DEPTH, B, D_MODEL), f32)
    z_wkv = jnp.zeros((DEPTH, B, N_HEADS, HEAD_SIZE, HEAD_SIZE), f32)
    z_pool = jnp.zeros((DEPTH, B, POOL_BUF, D_POOL), f32)
    z_conv = jnp.zeros((DEPTH, B, CONV_W - 1, 2 * D_FF), f32)
    y_p, shift_p, wkv_p, pool_p, conv_p = run_trunk(x_prompt, c_prompt, 0, z_shift, z_wkv, z_pool, z_conv, p)
    y_s, shift_s, wkv_s, pool_s, conv_s = run_trunk(x_sample, c_sample, PAST_LEN, state_shift, state_wkv,
                                                    state_pool, state_conv, p)
    dt = x_prompt.dtype
    return (y_p.astype(dt), y_s.astype(dt), shift_p.astype(dt), wkv_p.astype(dt), pool_p.astype(dt),
            conv_p.astype(dt), shift_s.astype(dt), wkv_s.astype(dt), pool_s.astype(dt), conv_s.astype(dt))


_drawn_inputs = setup_inputs


def setup_inputs(seed=0):
    import zlib

    import numpy as np

    out = dict(_drawn_inputs(seed))
    spreads = {}
    factors = {'decay_up': 8.0,
     'gn_w': 8.0,
     'gn_b': 64.0,
     'pool_scale': 4.643,
     'ln1_b': 5.223,
     'conv_b': 8.0,
     'ln2_b': 5.706,
     'r_k': 2.907}
    for name, (base, spread) in spreads.items():
        noise = np.random.default_rng([zlib.crc32(name.encode()), seed]).standard_normal(out[name].shape)
        drawn = base * np.exp(spread * noise) if base else spread * noise
        out[name] = __import__('jax').numpy.asarray(drawn.astype(out[name].dtype))
    for name, factor in factors.items():
        out[name] = (out[name] * factor).astype(out[name].dtype)
    return out
```

```python
from contextlib import ExitStack

import concourse.bass as bass
import numpy as np
from concourse import mybir

F32 = mybir.dt.float32
F32R = mybir.dt.float32r
ALU = mybir.AluOpType
ACT = mybir.ActivationFunctionType
AX = mybir.AxisListType

P = 128
D = 1024
KT = D // P
T = 512
NS = 8
TN = T + NS
TC = TN + NS
HC = TC // 2
NMOD = 1 + NS
H = 16
HD = 64
C = 64
NJ = T // C
NPOOL = 4
PB = 15
FF = 2816
FT = FF // P
DSH = 3 * D + 256
ALPHA = 2.0 ** 0.25
LN_EPS = 1e-5
GN_EPS = 64e-5
DECAY = float(np.exp(-0.5))
LEVELS = 6

C_ID = 0
C_BO = 128
C_MI = 256
C_MS = 320
C_MN = 384
C_OFF = 448
C_I2 = C_OFF + 64 * LEVELS
C_SC = C_I2 + 64
C_IC = C_SC + T
C_EPS = C_IC + 16 * NPOOL
C_END = C_EPS + 2


def shape_constants():
    c = np.zeros((P, C_END), np.float32)
    p = np.arange(P)[:, None]
    i = p % C
    t = np.arange(C)[None, :]
    c[:, C_ID:C_ID + P] = np.eye(P)
    c[:, C_BO:C_BO + P] = (p // HD) == (np.arange(P)[None, :] // HD)
    c[:, C_MI:C_MI + C] = i <= t
    c[:, C_MS:C_MS + C] = i < t
    c[:, C_MN:C_MN + C] = -(i < t).astype(np.float32)
    for lv in range(LEVELS):
        n = 1 << lv
        c[:, C_OFF + C * lv:C_OFF + C * (lv + 1)] = (i // (2 * n) == t // (2 * n)) & (i // n % 2 == 0) & (t // n % 2 == 1)
    c[:, C_I2:C_I2 + C] = i == t
    c[:, C_SC:C_SC + T] = (np.arange(T) % C != 0)[None, :]
    for g in range(NPOOL):
        w = 2 << g
        c[:, C_IC + 16 * g:C_IC + 16 * (g + 1)] = w / np.minimum(w, np.arange(16) + 1)[None, :]
    c[:, C_EPS] = LN_EPS
    c[:, C_EPS + 1] = GN_EPS
    return c


R_MU, R_W0, R_A0, R_KK, R_KA, R_RK, R_GW, R_GB = 0, 24, 32, 40, 48, 56, 64, 72
R_ML, R_PS = 80, 82
NPC = 10
Q_MU, Q_W0, Q_A0, Q_KK, Q_KA, Q_RK, Q_GW, Q_GB = 0, 3, 4, 5, 6, 7, 8, 9

B_LORA, B_RKV, B_POOL, B_BR, B_OUT, B_FF, B_DN = 0, 2, 26, 30, 62, 70, 114
ADA = 6 * KT


def rkv_slot(q):
    return (B_RKV + q) % 3


def pool_slot(q):
    return (B_POOL + q) % 3


def build(nc, i, o):
    es = ExitStack()
    with es:
        sems = {}

        def S(name):
            if name not in sems:
                sems[name] = es.enter_context(nc.semaphore(name))
            return sems[name]

        def sb(name, shape, dt=F32, ctx=es):
            return ctx.enter_context(nc.sbuf_tensor(name, shape, dt))

        def after(eng, name, n):
            if not isinstance(n, int) or n > 0:
                eng.wait_ge(S(name), n)

        def settle(eng):
            eng.sem_inc(S("settled"), 1)

        PJ = [es.enter_context(nc.psum_tensor(f"PJ{k}", [P, 2, 512], F32)) for k in range(2)]
        BB = es.enter_context(nc.psum_tensor("BB", [P, 4, 512], F32))
        B = [BB[:, k, :] for k in range(4)]

        CST = sb("CST", [P, C_END])
        PV = sb("PV", [P, 4, P])
        MOD = sb("MOD", [P, ADA, NMOD])
        Hh = sb("Hh", [P, KT, TC], F32R)
        Hl = sb("Hl", [P, KT, TC], F32R)
        RAW = sb("RAW", [P, 4, KT, P])
        Wh = sb("Wh", [P, 4, KT, P], F32R)
        Wl = sb("Wl", [P, 4, KT, P], F32R)
        SMP = sb("SMP", [P, KT, 6, NS])
        GS = sb("GS", [P, KT, NS])
        PLS = sb("PLS", [P, NPOOL, 16, NS])
        SCV = sb("SCV", [P, 2 * FT, NS, 2])
        UO = sb("UO", [P, 2 * FT, 2 + NS])
        G2 = sb("G2", [P, 2, NMOD])
        ACC = sb("ACC", [P, 4 * (2 + TN) + 4 * TN])
        YG = ACC[:, 0:KT * TN].rearrange("p (c t) -> p c t", c=KT)
        MO1 = YG
        FD = YG
        U = [[ACC[:, (2 * r + q) * (2 + TN):(2 * r + q + 1) * (2 + TN)] for q in range(2)] for r in range(2)]
        CV = [[ACC[:, 4 * (2 + TN) + (2 * r + q) * TN:4 * (2 + TN) + (2 * r + q + 1) * TN] for q in range(2)] for r in range(2)]
        ident = CST[:, C_ID:C_ID + P]
        bones = CST[:, C_BO:C_BO + P]

        w_in = i["w_in"][0].rearrange("(k p) e -> p k e", p=P)
        wsrc = {
            "in": w_in,
            "rwkv": i["w_branch_rwkv"][0].rearrange("(k p) e -> p k e", p=P),
            "pool": i["w_branch_pool"][0].rearrange("(k p) e -> p k e", p=P),
            "out": i["w_out"][0].rearrange("(k p) e -> p k e", p=P),
            "up": i["ffn_up"][0].rearrange("(k p) e -> p k e", p=P),
            "down": i["ffn_down"][0].rearrange("(k p) e -> p k e", p=P),
            "ada": i["ada_w"][0].rearrange("(k p) e -> p k e", p=P),
        }

        def cols(w, e, k0=0, kn=KT):
            return wsrc[w][:, k0:k0 + kn, bass.ds(e * P, P)] if not isinstance(e, int) else wsrc[w][:, k0:k0 + kn, e * P:(e + 1) * P]

        BR_KN = (KT, KT, KT, NPOOL)
        DN_KN = (8, 8, FT - 16)

        def br_src(e, q):
            return (cols("in", 30 + e), cols("in", 38 + e), cols("rwkv", e), cols("pool", e, 0, NPOOL))[q]

        def ff_src(m, q):
            return cols("up", 2 * m + q // 2 + FT * (q % 2))

        def dn_src(e, q):
            return cols("down", e, 8 * q, DN_KN[q])

        pool_loads = [16 * n for n in (9, 10, 10, 10)]
        br_loads = [16 * n for n in (11, 11, 11, 1)]
        ff_loads = [n + 160 for n in br_loads]

        def w_load(sp, n, slot, src, kn=KT, ring=3):
            after(sp, "w_lo", n + 1 - ring)
            sp.dma_start(RAW[:, slot, 0:kn, :], src).then_inc(S(f"w_load{slot}"), 16)

        def kstep(pe, out, slot, kw, xh, xl, kx, first, last, nb=(HC, HC)):
            for w, x in ((Wh, xh), (Wh, xl), (Wl, xh)):
                c0 = 0
                for b in range(2):
                    mm = pe.matmul(out[:, b, 0:nb[b]], w[:, slot, kw, :], x[:, kx, c0:c0 + nb[b]],
                                   start=first and w is Wh and x is xh, stop=last and w is Wl)
                    c0 += nb[b]
            return mm

        with ExitStack() as sc:
            PR = sb("PR", [P, 4, P], ctx=sc)
            XT = sb("XT", [P, 5, D], ctx=sc)
            XN = XT
            CT0 = sb("CT0", [NMOD, D], ctx=sc)
            SH0 = sb("SH0", [NS, D], ctx=sc)
            CT = sb("CT", [P, KT, NMOD], ctx=sc)
            BST = sb("BST", [P, 2, 6], ctx=sc)
            MV = sb("MV", [P, 5, 2], ctx=sc)
            SD = sb("SD", [P, 5], ctx=sc)
            RS = sb("RS", [P, 5], ctx=sc)
            Hf = sb("Hf", [P, KT, TC], ctx=sc)
            SHO = sb("SHO", [NMOD, D], ctx=sc)
            SP0 = sb("SP0", [NS * PB, NPOOL * P], ctx=sc)
            SC0 = sb("SC0", [2 * NS, 2 * FF], ctx=sc)
            MR = SHO[:].rearrange("p (a b) -> p a b", a=2)
            AW = (RAW[:].rearrange("p a k d -> p (a k d)").rearrange("p (k d) -> p k d", k=KT),
                  ACC[:, 0:4 * KT * P].rearrange("p (k d) -> p k d", k=KT))

            def ada_src(q):
                return wsrc["ada"][:, :, bass.ds(q * 4 * P, 4 * P)]

            block = sc.enter_context(nc.Block())

            @block.sync
            def _(sp):
                sp.dma_start(CST[:], i["consts"]).then_inc(S("ld_cst"), 16)
                sp.dma_start(CT0[0:1, :], i["c_prompt"]).then_inc(S("ld_c"), 16)
                sp.dma_start(CT0[1:NMOD, :], i["c_sample"]).then_inc(S("ld_c"), 16)
                for b in range(2):
                    sp.dma_start(AW[b], ada_src(b)).then_inc(S(f"ld_ada{b}"), 16)
                g0 = [("mu_shift", R_MU, 24, 0), ("decay_w0", R_W0, 8, 0), ("aaa_a0", R_A0, 8, 0), ("k_k", R_KK, 8, 0),
                      ("k_a", R_KA, 8, 0), ("gn_w", R_GW, 8, 0), ("gn_b", R_GB, 8, 0), ("pool_scale", R_PS, 4, 0),
                      ("mu_shift", R_ML, 2, 24)]
                for name, r, n, s in g0:
                    sp.dma_start(PR[r:r + n, 0, :], i[name][0][s * P:(s + n) * P].rearrange("(n p) -> n p", p=P)).then_inc(S("ld_par"), 16)
                sp.dma_start(PR[R_RK:R_RK + 8, 0, :], i["r_k"][0].rearrange("(n a) d -> n (a d)", a=2)).then_inc(S("ld_par"), 16)
                sp.dma_start(PR[0:ADA, 1, :], i["ada_b"][0].rearrange("(n p) -> n p", p=P)).then_inc(S("ld_par"), 16)
                sp.dma_start(PR[ADA:ADA + 44, 1, :], i["conv_b"][0].rearrange("(n p) -> n p", p=P)).then_inc(S("ld_par"), 16)
                for k in range(2):
                    sp.dma_start(PR[44 * k:44 * k + 44, 2, :], i["conv_w"][0, k].rearrange("(n p) -> n p", p=P)).then_inc(S("ld_par"), 16)
                sp.dma_start(PR[0:44, 3, :], i["conv_w"][0, 2].rearrange("(n p) -> n p", p=P)).then_inc(S("ld_par"), 16)
                sp.dma_start(XT[:, 0:4, :], i["x_prompt"][0].rearrange("(a p) d -> p a d", p=P)).then_inc(S("ld_x"), 16)
                sp.dma_start(XT[0:NS, 4, :], i["x_sample"][:, 0, :]).then_inc(S("ld_x"), 16)
                sp.dma_start(SH0[:], i["state_shift"][0]).then_inc(S("ld_st"), 16)
                sp.dma_start(SP0[:], i["state_pool"][0].rearrange("b t d -> (b t) d")).then_inc(S("ld_st"), 16)
                sp.dma_start(SC0[:], i["state_conv"][0].rearrange("b t d -> (b t) d")).then_inc(S("ld_st"), 16)
                sp.dma_start(o["pool_s"][0, :, 0:PB - 1, :], i["state_pool"][0, :, 1:PB, :]).then_inc(S("out"), 16)
                sp.dma_start(o["conv_s"][0, :, 0, :], i["state_conv"][0, :, 1, :]).then_inc(S("out"), 16)
                with sp.Fori(1, ADA // 8) as q2:
                    for b in range(2):
                        sp.wait_ge(S("ada_used"), 2 * q2 + b - 1)
                        sp.dma_start(AW[b], ada_src(2 * q2 + b)).then_inc(S(f"ld_ada{b}"), 16)
                sp.wait_ge(S("sho"), 1)
                sp.dma_start(o["shift_p"][0], SHO[0:1, :]).then_inc(S("out"), 16)
                sp.dma_start(o["shift_s"][0], SHO[1:NMOD, :]).then_inc(S("out"), 16)

            @block.tensor
            def _(pe):
                pe.wait_ge(S("ld_cst"), 16)
                pe.wait_ge(S("ld_c"), 32)
                for k in range(KT):
                    mm = pe.transpose(B[0][:, k * NMOD:(k + 1) * NMOD], CT0[:, k * P:(k + 1) * P], ident[0:NMOD, 0:NMOD])
                mm.then_inc(S("t_c"), 1)
                pe.wait_ge(S("ld_par"), 16 * 15)
                for g, n in enumerate((86, 92, 88, 44)):
                    mm = pe.transpose(B[1][:, g * P:g * P + n], PR[0:n, g, :], ident[0:n, 0:n])
                mm.then_inc(S("t_par"), 1)
                pe.wait_ge(S("ct"), 1)
                pe.wait_ge(S("chain"), 2)

                def rows(q, b):
                    pe.wait_ge(S(f"ld_ada{b}"), (q - b) * 8 + 16)
                    after(pe, "mod_rows", q - 1)
                    settle(pe)
                    for k in range(KT):
                        mm = pe.matmul(B[2 + b][0:NMOD, :], CT[:, k, :], AW[b][:, k, :], start=k == 0, stop=k == KT - 1)
                    mm.then_inc(S("ada_used"), 1)

                def turn(q, b):
                    pe.wait_ge(S("mod_rows"), q + 1)
                    after(pe, "mod", q - 1)
                    settle(pe)
                    for s in range(4):
                        mm = pe.transpose(B[b][:, s * NMOD:(s + 1) * NMOD], MR[:, b, s * P:(s + 1) * P], ident[0:NMOD, 0:NMOD])
                    mm.then_inc(S("t_mod"), 1)

                rows(0, 0)
                rows(1, 1)
                turn(0, 0)
                with pe.Fori(1, ADA // 8) as q2:
                    rows(2 * q2, 0)
                    turn(2 * q2 - 1, 1)
                    rows(2 * q2 + 1, 1)
                    turn(2 * q2, 0)
                turn(ADA // 4 - 1, 1)
                pe.wait_ge(S("mod"), ADA // 4)
                pe.wait_ge(S("xn"), 5)
                for k in range(KT):
                    after(pe, "hf", k - 1)
                    for t in range(4):
                        mm = pe.transpose(B[k % 2][:, t * P:(t + 1) * P], XN[:, t, k * P:(k + 1) * P], ident)
                    mm.then_inc(S("t_x"), 1)
                pe.wait_ge(S("ld_st"), 48)
                for k in range(KT):
                    mm = pe.transpose(B[2][:, k * NS:(k + 1) * NS], XN[0:NS, 4, k * P:(k + 1) * P], ident[0:NS, 0:NS])
                    mm = pe.transpose(B[3][:, k * NS:(k + 1) * NS], SH0[:, k * P:(k + 1) * P], ident[0:NS, 0:NS])
                mm.then_inc(S("t_s"), 1)
                for g in range(NPOOL):
                    mm = pe.transpose(PJ[0][:, 0, g * P:g * P + NS * PB], SP0[:, g * P:(g + 1) * P], ident[0:NS * PB, 0:NS * PB])
                for f in range(2 * FT):
                    b, r = divmod(f, 22)
                    mm = pe.transpose(PJ[1][:, b, r * 16:(r + 1) * 16], SC0[:, f * P:(f + 1) * P], ident[0:16, 0:16])
                mm.then_inc(S("t_st"), 1)
                pe.wait_ge(S("hf"), KT + 1)
                pe.wait_ge(S("st_in"), 1)
                for k in range(KT):
                    b, r = divmod(k, 4)
                    mm = pe.transpose(PJ[0][0:NMOD, b, r * P:(r + 1) * P], Hf[:, k, T - 1:TN], ident)
                mm.then_inc(S("t_sho"), 1)

            @block.scalar
            def _(act):
                act.wait_ge(S("t_c"), 1)
                act.activation(CT[:].rearrange("p a b -> p (a b)"), B[0][:, 0:KT * NMOD], ACT.Copy).then_inc(S("ct"), 1)
                def mod_rows(q, b):
                    act.wait_ge(S("ada_used"), q + 1)
                    after(act, "t_mod", q - 1)
                    act.activation(MR[:, b, :], B[2 + b][0:NMOD, :], ACT.Copy).then_inc(S("mod_rows"), 1)

                mod_rows(0, 0)
                mod_rows(1, 1)
                act.wait_ge(S("mv"), 5)
                act.activation(SD[:], MV[:, :, 1], ACT.Sqrt, bias=CST[:, C_EPS:C_EPS + 1]).then_inc(S("sd"), 1)
                with act.Fori(1, ADA // 8) as q2:
                    for b in range(2):
                        mod_rows(2 * q2 + b, b)
                act.wait_ge(S("mod1"), 2)
                for k in range(KT):
                    act.wait_ge(S("t_x"), k + 1)
                    act.activation(Hf[:, k, 0:T], B[k % 2], ACT.Identity, bias=MOD[:, k, 0:1],
                                   scale=MOD[:, KT + k, 0:1]).then_inc(S("hf"), 1)
                for k in range(KT):
                    act.wait_ge(S("hf"), KT + 1)
                    act.activation(Hh[:, k, :], Hf[:, k, :], ACT.Copy).then_inc(S("hh"), 1)
                act.wait_ge(S("t_sho"), 1)
                act.activation(SHO[:].rearrange("p (a b) -> p a b", a=2), PJ[0][0:NMOD, :, :], ACT.Copy).then_inc(S("sho"), 1)

            @block.vector
            def _(dve):
                dve.memset(MV[:], 1.0).then_inc(S("chain"), 1)
                dve.wait_ge(S("t_par"), 1)
                for g, n in enumerate((86, 92, 88, 44)):
                    pv = dve.tensor_copy(PV[:, g, 0:n], B[1][:, g * P:g * P + n])
                pv.then_inc(S("chain"), 1)
                dve.wait_ge(S("chain"), 2)
                dve.wait_ge(S("ld_x"), 32)
                dve.wait_ge(S("chain"), 1)
                for t in range(5):
                    n = P if t < 4 else NS
                    after(dve, "mv", t)
                    for b in range(2):
                        bs = dve.bn_stats(BST[0:n, b, :], XT[0:n, t, b * 512:(b + 1) * 512])
                    bs.then_inc(S("chain"), 1)
                    dve.wait_ge(S("chain"), t + 3)
                    dve.bn_aggr(MV[0:n, t, :], BST[0:n].rearrange("p a b -> p (a b)")).then_inc(S("mv"), 1)
                dve.wait_ge(S("sd"), 1)
                dve.reciprocal(RS[:], SD[:]).then_inc(S("chain"), 1)
                dve.wait_ge(S("chain"), 8)
                for t in range(5):
                    n = P if t < 4 else NS
                    dve.tensor_scalar(XN[0:n, t, :], XT[0:n, t, :], MV[0:n, t, 0:1], RS[0:n, t:t + 1],
                                      ALU.subtract, ALU.mult).then_inc(S("xn"), 1)
                with dve.Fori(0, ADA // 8) as q2:
                    for b in range(2):
                        dve.wait_ge(S("t_mod"), 2 * q2 + b + 1)
                        dve.tensor_tensor(MOD[:, bass.ds(8 * q2 + 4 * b, 4), :], B[b][:, 0:4 * NMOD].rearrange("p (a b) -> p a b", a=4),
                                          PV[:, 1, bass.ds(8 * q2 + 4 * b, 4)].unsqueeze(2).to_broadcast([P, 4, NMOD]), ALU.add).then_inc(S("mod"), 1)
                dve.wait_ge(S("mod"), ADA // 4)
                for a in (KT, 4 * KT):
                    dve.tensor_scalar(MOD[:, a:a + 2 * KT, :], MOD[:, a:a + 2 * KT, :], 1.0, None, ALU.add).then_inc(S("mod1"), 1)
                dve.wait_ge(S("mod1"), 2)
                dve.wait_ge(S("t_s"), 1)
                smp = B[2][:, 0:KT * NS].rearrange("p (a b) -> p a b", a=KT)
                dve.tensor_tensor(Hf[:, :, T:TN], smp, MOD[:, KT:2 * KT, 1:NMOD], ALU.mult).then_inc(S("chain"), 1)
                dve.tensor_copy(Hf[:, :, TN:TC], B[3][:, 0:KT * NS].rearrange("p (a b) -> p a b", a=KT))
                dve.wait_ge(S("chain"), 9)
                dve.tensor_tensor(Hf[:, :, T:TN], Hf[:, :, T:TN], MOD[:, 0:KT, 1:NMOD], ALU.add).then_inc(S("hf"), 1)
                dve.wait_ge(S("t_st"), 1)
                for g in range(NPOOL):
                    dve.tensor_copy(PLS[:, g, 0:PB, :].rearrange("p t b -> p b t"),
                                    PJ[0][:, 0, g * P:g * P + NS * PB].rearrange("p (b t) -> p b t", b=NS))
                for b in range(2):
                    st = dve.tensor_copy(SCV[:, 22 * b:22 * b + 22].rearrange("p f b t -> p f (b t)"),
                                         PJ[1][:, b, 0:352].rearrange("p (f b) -> p f b", f=22))
                st.then_inc(S("st_in"), 1)
                for k in range(KT):
                    dve.wait_ge(S("hh"), k + 1)
                    dve.tensor_tensor(Hl[:, k, :], Hf[:, k, :], Hh[:, k, :].bitcast(F32), ALU.subtract)
        HH = [slice(0, HD), slice(HD, P)]
        BKT_OF = {0: slice(1, 3), 1: slice(0, 2)}
        with ExitStack() as sc:
            WL = sb("WL", [P, P], ctx=sc)
            WG = sb("WG", [P, P], ctx=sc)
            TWA = sb("TWA", [P, TN], ctx=sc)
            SGL = sb("SGL", [P, TN], ctx=sc)
            A1 = sb("A1", [P, TC], ctx=sc)
            A2 = sb("A2", [P, 1 + TC], ctx=sc)
            PCT = sb("PCT", [P, NPC], ctx=sc)
            OM = sb("OM", [P, 5], ctx=sc)
            PCN = sb("PCN", [P, NPC], ctx=sc)
            XR = sb("XR", [P, TN], ctx=sc)
            XK = sb("XK", [P, TN], ctx=sc)
            VX = sb("VX", [P, C + TN], ctx=sc)
            SW = sb("SW", [P, TN], ctx=sc)
            AL = sb("AL", [P, TN], ctx=sc)
            G = sb("G", [P, TN], ctx=sc)
            LC = sb("LC", [P, T], ctx=sc)
            PP = sb("PP", [P, NJ, C + 1], ctx=sc)
            PI = sb("PI", [P, T], ctx=sc)
            KN = sb("KN", [P, TN], ctx=sc)
            KKN = sb("KKN", [P, TN], ctx=sc)
            SM = sb("SM", [P, TN], ctx=sc)
            K2 = sb("K2", [P, TN], ctx=sc)
            KB = sb("KB", [P, TN], ctx=sc)
            BV = sb("BV", [P, T], ctx=sc)
            AR = sb("AR", [P, 2, T], ctx=sc)
            BK = sb("BK", [P, NJ, 3, C], ctx=sc)
            RHO = sb("RHO", [P, T], ctx=sc)
            GH = sb("GH", [P, 2, NJ, C], ctx=sc)
            AN = sb("AN", [P, 2, NJ, C], ctx=sc)
            MT = sb("MT", [P, NJ, C], ctx=sc)
            MO = sb("MO", [P, 2, NJ, C], ctx=sc)
            TI = sb("TI", [P, NJ, C], ctx=sc)
            TT = sb("TT", [P, NJ, C], ctx=sc)
            XI = sb("XI", [P, NJ, C], ctx=sc)
            BT = sb("BT", [P, 2, NJ, C], ctx=sc)
            Z = sb("Z", [P, 2, NJ, C], ctx=sc)
            SV = sb("SV", [P, 2, NJ + 1, C], ctx=sc)
            RS1 = sb("RS1", [P, C], ctx=sc)
            YF = sb("YF", [P, T], ctx=sc)
            YQ = sb("YQ", [P, T], ctx=sc)
            WK = sb("WK", [C, 2, C], ctx=sc)
            I2 = CST[:, C_I2:C_I2 + C]
            block = sc.enter_context(nc.Block())

            def rows8(m):
                return m.unsqueeze(1).to_broadcast([P, NJ, C])

            def by8(m):
                return m[:, 0:T].rearrange("p (j t) -> p j t", j=NJ)

            TSTEPS = (1, 2, 1, 2, 1, 2, 1, 2, 1, 2, 1)

            @block.sync
            def _(sp):
                def block_in(n, slot, e):
                    if isinstance(n, int) and n < 3:
                        sp.dma_start(RAW[:, slot], cols("in", e)).then_inc(S(f"w_load{slot}"), 16)
                    else:
                        w_load(sp, n, slot, cols("in", e))

                def lora_up(c):
                    if not isinstance(c, int) or c > 0:
                        sp.wait_ge(S("mm_g"), c)
                    at = bass.ds(c * P, P)
                    sp.dma_start(WL[0:64, :], i["decay_up"][0][:, at]).then_inc(S("ld_up"), 16)
                    sp.dma_start(WL[64:P, :], i["aaa_up"][0][:, at]).then_inc(S("ld_up"), 16)
                    sp.dma_start(WG[:], i["gate_up"][0][:, at]).then_inc(S("ld_up"), 16)

                def wkv_out(c):
                    sp.wait_ge(S("wk"), c + 1)
                    sp.dma_start(o["wkv_p"][0, 0, bass.ds(2 * c, 2)].rearrange("h v k -> v h k"), WK[:]).then_inc(S("wk_out"), 16)

                for q in range(2):
                    block_in(q, q, 24 + q)
                for q in range(3):
                    block_in(B_RKV + q, rkv_slot(q), KT * q)
                lora_up(0)
                for q in range(3):
                    block_in(B_RKV + 3 + q, rkv_slot(q), KT * q + 1)
                with sp.Fori(1, KT - 1) as c:
                    lora_up(c)
                    wkv_out(c - 1)
                    for q in range(3):
                        block_in(B_RKV + 3 * (c + 1) + q, rkv_slot(q), c + 1 + KT * q)
                lora_up(KT - 1)
                wkv_out(KT - 2)
                wkv_out(KT - 1)
                sp.wait_ge(S("wk_out"), 16 * KT)

            @block.tensor
            def _(pe):
                def project(n, slot, pj, k0, k1):
                    if k0 == 0:
                        pe.wait_ge(S("w_lo"), n + 1)
                    for k in range(k0, k1):
                        mm = kstep(pe, PJ[pj], slot, k, Hh, Hl, k, k == 0, k == KT - 1)
                    if k1 == KT:
                        mm.then_inc(S("prj"), 1)

                def project_upto(c, done, upto):
                    for st in range(done, upto):
                        q, k = divmod(st, KT)
                        n = B_RKV + 3 * c + q
                        if k == 0:
                            pe.wait_ge(S("w_lo"), n + 1)
                            pe.wait_ge(S("prj_ev"), n - 1)
                            if q == 0:
                                after(pe, "ssm", c)
                            if q == 1:
                                after(pe, "bv", c)
                        mm = kstep(pe, PJ[q % 2], rkv_slot(q), k, Hh, Hl, k, k == 0, k == KT - 1)
                        if k == KT - 1:
                            mm.then_inc(S("prj"), 1)

                def small(out, w, x, n, half):
                    for b in range(2):
                        mm = pe.matmul(out[:, b, 0:half], w, x[:, b * half:(b + 1) * half], start=True, stop=True)
                    return mm

                def tile(c, more):
                    pe.wait_ge(S("ld_up"), 48 * (c + 1))
                    pe.wait_ge(S("prj_ev"), B_RKV + 3 * c + 2)
                    after(pe, "gsd", c)
                    pe.wait_ge(S("twa"), 2)
                    small(PJ[1], WL[0:64, :], TWA[0:64, :], 64, 260).then_inc(S("mm_zw"), 1)
                    pe.wait_ge(S("prj_ev"), B_RKV + 3 * c + 3)
                    small(PJ[0], WL[64:P, :], TWA[64:P, :], 64, 260).then_inc(S("mm_za"), 1)
                    pe.wait_ge(S("sigw"), c + 1)
                    small(PJ[1], WG[:], SGL[:], P, 260).then_inc(S("mm_g"), 1)
                    pe.wait_ge(S("alpha"), c + 1)
                    pe.wait_ge(S("kks"), c + 1)
                    small(PJ[0], bones, KN[:], P, 260).then_inc(S("mm_ss"), 1)
                    pe.wait_ge(S("gte"), c + 1)
                    pe.wait_ge(S("rk2"), c + 1)
                    small(PJ[1], bones, SM[:], P, 260).then_inc(S("mm_bo"), 1)
                    pe.wait_ge(S("ar"), c + 1)
                    pe.wait_ge(S("kap"), c + 1)
                    after(pe, "yf", 2 * c)
                    after(pe, "wk", c)
                    for jj in range(2):
                        for h in range(2):
                            for j in range(4):
                                t0 = (4 * jj + j) * C
                                mm = pe.matmul(B[2 * jj + h][:, j * P:(j + 1) * P], BK[HH[h], 4 * jj + j, BKT_OF[h], :].rearrange("p s t -> p (s t)"),
                                               AR[HH[h], :, t0:t0 + C], start=True, stop=True)
                        mm.then_inc(S("gram"), 1)
                    pe.wait_ge(S("gram_ev"), 2 * c + 2)
                    settle(pe)
                    for h in range(2):
                        for j in range(NJ):
                            if h == 0:
                                mm = pe.transpose(B[0][:, j * C:(j + 1) * C], VX[0:64, j * C:(j + 2) * C], ident[0:64, 0:64])
                            else:
                                mm = pe.transpose(B[1][0:64, j * C:(j + 1) * C], VX[64:P, (j + 1) * C:(j + 2) * C], ident[64:P, 64:P])
                    mm.then_inc(S("t_v"), 1)
                    pe.wait_ge(S("bke"), c + 1)
                    settle(pe)
                    for h in range(2):
                        for j in range(NJ):
                            mm = pe.transpose(B[2 + h][:, j * C:(j + 1) * C], BK[HH[h], j, BKT_OF[h], :].rearrange("p s t -> p (s t)"),
                                              ident[HH[h], HH[h]])
                    mm.then_inc(S("t_bk"), 1)
                    done = 0
                    g = 0
                    for lv in range(LEVELS):
                        pe.wait_ge(S("mo"), LEVELS * c + lv + 1)
                        if lv == 0:
                            pe.wait_ge(S("v_ev"), 2 * c + 2)
                            pe.wait_ge(S("bt_ev"), 2 * c + 2)
                        elif lv == 1:
                            pe.wait_ge(S("ti_1"), c + 1)
                        else:
                            pe.wait_ge(S("ti"), (LEVELS - 2) * c + lv - 1)
                        settle(pe)
                        for h in range(2):
                            for j in range(NJ):
                                mm = pe.matmul(B[h][HH[h], j * C:(j + 1) * C], MO[HH[h], lv % 2, j, :],
                                               I2[HH[h], :] if lv == 0 else TI[HH[h], j, :], start=True, stop=True)
                        mm.then_inc(S("mm_x"), 1)
                        if more:
                            project_upto(c + 1, done, done + TSTEPS[g])
                            done += TSTEPS[g]
                        g += 1
                        if lv == 0:
                            continue
                        if lv == 1:
                            pe.wait_ge(S("tt_1"), c + 1)
                        else:
                            pe.wait_ge(S("tt0"), (LEVELS - 1) * c + lv - 1)
                            pe.wait_ge(S("tt1"), (LEVELS - 1) * c + lv - 1)
                        pe.wait_ge(S("xi"), (LEVELS - 1) * c + lv)
                        settle(pe)
                        if lv < LEVELS - 1:
                            for h in range(2):
                                for j in range(NJ):
                                    mm = pe.matmul(B[h][HH[h], j * C:(j + 1) * C], TT[HH[h], j, :], XI[HH[h], j, :], start=True, stop=True)
                            mm.then_inc(S("mm_ti"), 1)
                        for h in range(2):
                            for j in range(NJ):
                                mm = pe.matmul(B[2 + h][HH[h], j * C:(j + 1) * C], XI[HH[h], j, :], TT[HH[h], j, :], start=True, stop=True)
                        mm.then_inc(S("mm_tt"), 1)
                        if more:
                            project_upto(c + 1, done, done + TSTEPS[g])
                            done += TSTEPS[g]
                        g += 1
                    pe.wait_ge(S("tt0"), (LEVELS - 1) * (c + 1))
                    pe.wait_ge(S("tt1"), (LEVELS - 1) * (c + 1))

                    def outputs(j):
                        for h in range(2):
                            pe.matmul(B[2 + h][HH[h], j * C:(j + 1) * C], Z[:, h, j, :], GH[:, h, j, :], start=True, stop=False)
                        for h in range(2):
                            mm = pe.matmul(B[2 + h][HH[h], j * C:(j + 1) * C], SV[HH[h], h, j, :], RHO[HH[h], j * C:(j + 1) * C],
                                           start=False, stop=True)
                        return mm

                    for j in range(NJ):
                        if j > 0:
                            pe.wait_ge(S("s"), NJ * c + j)
                        for h in range(2):
                            mm = pe.matmul(B[0][HH[h], 0:C], AN[:, h, j, :], SV[:, h, j, :], start=True, stop=True)
                        mm.then_inc(S("mm_r"), 1)
                        if j > 0:
                            outputs(j - 1)
                        pe.wait_ge(S("r"), NJ * c + j + 1)
                        settle(pe)
                        for h in range(2):
                            mm = pe.matmul(B[h][HH[h], 2 * C:3 * C], TT[HH[h], j, :], RS1[HH[h], :], start=True, stop=True)
                        mm.then_inc(S("mm_u"), 1)
                        if more:
                            project_upto(c + 1, done, done + 1)
                            done += 1
                        pe.wait_ge(S("u0"), NJ * c + j + 1)
                        pe.wait_ge(S("u1"), NJ * c + j + 1)
                        for h in range(2):
                            mm = pe.matmul(B[0][HH[h], C:2 * C], BT[:, h, j, :], Z[:, h, j, :], start=True, stop=True)
                        mm.then_inc(S("mm_s"), 1)
                    outputs(NJ - 1).then_inc(S("mm_y"), 1)
                    pe.wait_ge(S("s"), NJ * c + NJ)
                    settle(pe)
                    for h in range(2):
                        mm = pe.transpose(B[h][0:C, 0:C], SV[HH[h], h, NJ, :], ident[HH[h], HH[h]])
                    mm.then_inc(S("t_wk"), 1)
                    pe.wait_ge(S("yf"), 2 * c + 2)
                    if more:
                        pe.wait_ge(S("prj_ev"), B_RKV + 3 * (c + 1) + 2)
                    small(PJ[1], bones, YF[:], P, 256).then_inc(S("mm_mu"), 1)
                    pe.wait_ge(S("yc"), c + 1)
                    pe.wait_ge(S("yq"), c + 1)
                    small(PJ[1], bones, YQ[:], P, 256).then_inc(S("mm_var"), 1)

                for n in range(2):
                    project(n, n, n, 0, KT)
                project_upto(0, 0, 24)
                tile(0, True)
                with pe.Fori(1, KT - 1) as c:
                    tile(c, True)
                tile(KT - 1, False)

            @block.scalar
            def _(act):
                def shift_in(n, pj, mu, om):
                    act.wait_ge(S("prj"), n + 1)
                    after(act, "xs", n)
                    act.activation(A1[:].rearrange("p (a b) -> p a b", a=2), PJ[pj][:, :, 0:HC], ACT.Copy, scale=om)
                    act.activation(A2[:, 1:1 + TC].rearrange("p (a b) -> p a b", a=2), PJ[pj][:, :, 0:HC], ACT.Copy,
                                   scale=mu).then_inc(S("prj_ev"), 1)

                def split(n, slot, loads):
                    act.wait_ge(S(f"w_load{slot}"), loads)
                    if not isinstance(n, int) or n >= 3:
                        act.wait_ge(S("prj"), n - 2)
                    act.activation(Wh[:, slot], RAW[:, slot], ACT.Copy).then_inc(S("w_hi"), 1)

                def loads(slot, c):
                    return 16 * ((1 if slot < 2 else 0) + c + 1)

                def tile(c, more):
                    two = lambda a: a.rearrange("p (a b) -> p a b", a=2)
                    act.wait_ge(S("mm_zw"), c + 1)
                    act.activation(two(SW[:]), PJ[1][:, :, 0:260], ACT.Sigmoid, bias=PCT[:, Q_W0:Q_W0 + 1]).then_inc(S("sigw"), 1)
                    act.wait_ge(S("mm_za"), c + 1)
                    act.activation(two(AL[:]), PJ[0][:, :, 0:260], ACT.Sigmoid, bias=PCT[:, Q_A0:Q_A0 + 1]).then_inc(S("alpha"), 1)
                    act.activation(KN[:], XK[:], ACT.Square, scale=PCT[:, Q_KK:Q_KK + 1]).then_inc(S("kks"), 1)
                    act.wait_ge(S("mm_g"), c + 1)
                    act.activation(two(G[:]), PJ[1][:, :, 0:260], ACT.Copy).then_inc(S("gte"), 1)
                    act.wait_ge(S("lc"), c + 1)
                    act.activation(PP[:, :, 1:C + 1], LC[:].rearrange("p (j t) -> p j t", j=NJ), ACT.Exp, scale=-DECAY)
                    act.activation(PI[:], LC[:], ACT.Exp, scale=DECAY).then_inc(S("pi"), 1)
                    act.activation(SMP[:, bass.ds(c, 1), 1, :].rearrange("p a b -> p (a b)"), SW[:, T:TN], ACT.Exp, scale=-DECAY)
                    act.wait_ge(S("ssm"), c + 1)
                    act.activation(KN[:], KN[:], ACT.Ln).then_inc(S("kn"), 1)
                    act.wait_ge(S("kn"), c + 1)
                    act.activation(KN[:], KN[:], ACT.Exp, scale=-0.5).then_inc(S("rn"), 1)
                    if more:
                        for q in range(3):
                            split(B_RKV + 3 * (c + 1) + q, rkv_slot(q), loads(rkv_slot(q), c + 1))
                    act.wait_ge(S("ar"), c + 1)
                    for h in range(2):
                        act.activation(AN[HH[h], h, :, :], AR[HH[h], 0, :].rearrange("p (j t) -> p j t", j=NJ), ACT.Copy)
                    act.wait_ge(S("t_v"), c + 1)
                    act.activation(Z[64:P, 0, :, :], B[0][64:P, :].rearrange("p (j t) -> p j t", j=NJ), ACT.Copy)
                    act.activation(SV[64:P, 0, 0:NJ, :], B[0][64:P, :].rearrange("p (j t) -> p j t", j=NJ), ACT.Copy).then_inc(S("v_ev"), 1)
                    act.wait_ge(S("t_bk"), c + 1)
                    act.activation(BT[:, 0, :, :], B[2].rearrange("p (j t) -> p j t", j=NJ), ACT.Copy).then_inc(S("bt_ev"), 1)
                    for lv in range(1, LEVELS):
                        if lv < LEVELS - 1:
                            act.wait_ge(S("mm_ti"), (LEVELS - 2) * c + lv)
                            for h in range(2):
                                cp = act.activation(TI[HH[h]], B[h][HH[h]].rearrange("p (j t) -> p j t", j=NJ), ACT.Copy)
                            cp.then_inc(S("ti"), 1)
                        act.wait_ge(S("mm_tt"), (LEVELS - 1) * c + lv)
                        act.activation(TT[HH[0]], B[2][HH[0]].rearrange("p (j t) -> p j t", j=NJ), ACT.Copy).then_inc(S("tt0"), 1)
                        if lv == LEVELS - 2 and more:
                            shift_in(B_RKV + 3 * (c + 1), 0, PCN[:, 0:1], OM[:, 0:1])
                    for j in range(NJ):
                        act.wait_ge(S("mm_u"), NJ * c + j + 1)
                        act.activation(Z[HH[1], 1, j, :], B[1][HH[1], 2 * C:3 * C], ACT.Copy, scale=-1.0).then_inc(S("u1"), 1)
                        if j == 1 and more:
                            shift_in(B_RKV + 3 * (c + 1) + 1, 1, PCN[:, 1:2], OM[:, 1:2])
                    act.wait_ge(S("mm_y"), c + 1)
                    act.activation(YF[HH[0], :], B[2][HH[0], :], ACT.Copy).then_inc(S("yf"), 1)
                    act.wait_ge(S("t_wk"), c + 1)
                    after(act, "wk_out", 16 * c)
                    for h in range(2):
                        w = act.activation(WK[:, h, :], B[h][0:C, 0:C], ACT.Copy)
                    w.then_inc(S("wk"), 1)
                    if more:
                        shift_in(B_RKV + 3 * (c + 1) + 2, 0, PCN[:, 2:3], OM[:, 2:3])
                    act.wait_ge(S("yc"), c + 1)
                    act.activation(YQ[:], YF[:], ACT.Square).then_inc(S("yq"), 1)
                    act.wait_ge(S("mm_var"), c + 1)
                    act.activation(YQ[:].rearrange("p (a b) -> p a b", a=2), PJ[1][:, :, 0:256], ACT.Ln,
                                   bias=CST[:, C_EPS + 1:C_EPS + 2], scale=1.0 / HD).then_inc(S("gsd"), 1)
                    act.wait_ge(S("gsd"), c + 1)
                    act.activation(YQ[:], YQ[:], ACT.Exp, scale=-0.5).then_inc(S("grs"), 1)

                split(0, 0, 16)
                split(1, 1, 16)
                act.wait_ge(S("om_l"), 1)
                shift_in(0, 0, PV[:, 0, R_ML:R_ML + 1], OM[:, 3:4])
                split(2, 2, 16)
                act.wait_ge(S("xl"), 1)
                act.activation(TWA[0:64, :], SW[0:64, :], ACT.Tanh).then_inc(S("twa"), 1)
                shift_in(1, 1, PV[:, 0, R_ML + 1:R_ML + 2], OM[:, 4:5])
                act.wait_ge(S("xl"), 2)
                act.activation(SGL[:], AL[:], ACT.Sigmoid).then_inc(S("twa"), 1)
                split(3, 0, 32)
                split(4, 1, 32)
                act.wait_ge(S("om"), 1)
                for q in range(3):
                    shift_in(B_RKV + q, q % 2, PCN[:, q:q + 1], OM[:, q:q + 1])
                act.wait_ge(S("pct"), 1)
                tile(0, True)
                with act.Fori(1, KT - 1) as c:
                    act.wait_ge(S("pct"), c + 1)
                    tile(c, True)
                act.wait_ge(S("pct"), KT)
                tile(KT - 1, False)

            @block.vector
            def _(dve):
                def lo(n, slot):
                    dve.wait_ge(S("w_hi"), n + 1)
                    dve.tensor_tensor(Wl[:, slot], RAW[:, slot], Wh[:, slot].bitcast(F32), ALU.subtract).then_inc(S("w_lo"), 1)

                def shift_add(n, out):
                    dve.wait_ge(S("prj_ev"), n + 1)
                    dve.tensor_tensor(out[:, 0:T], A1[:, 0:T], A2[:, 0:T], ALU.add)
                    return dve.tensor_tensor(out[:, T:TN], A1[:, T:TN], A2[:, 1 + TN:1 + TC], ALU.add)

                def params(c):
                    src = PV[:, 0, 0:NPC * KT].rearrange("p (q c) -> p q c", c=KT)[:, :, bass.ds(c, 1)].rearrange("p q c -> p (q c)")
                    dve.tensor_copy(PCN[:], src).then_inc(S("pcn"), 1)
                    dve.wait_ge(S("pcn"), c + 1)
                    dve.tensor_scalar(OM[:, 0:3], PCN[:, 0:3], -1.0, 1.0, ALU.mult, ALU.add).then_inc(S("om"), 1)

                def adopt(c):
                    dve.wait_ge(S("om"), c + 1)
                    dve.tensor_copy(PCT[:], PCN[:]).then_inc(S("pct"), 1)

                def tile(c, more):
                    dve.wait_ge(S("sigw"), c + 1)
                    dve.tensor_tensor_scan(LC[:], CST[:, C_SC:C_SC + T], SW[:, 0:T], 0.0, ALU.mult, ALU.add).then_inc(S("lc"), 1)
                    dve.wait_ge(S("alpha"), c + 1)
                    dve.wait_ge(S("pct"), c + 1)
                    dve.tensor_scalar(KB[:], AL[:], -1.0, PCT[:, Q_KA:Q_KA + 1], ALU.add, ALU.mult).then_inc(S("k_chain"), 1)
                    dve.wait_ge(S("k_chain"), 2 * c + 1)
                    dve.scalar_tensor_tensor(K2[:], KB[:], 1.0, XK[:], ALU.add, ALU.mult).then_inc(S("k_chain"), 1)
                    dve.wait_ge(S("k_chain"), 2 * c + 2)
                    dve.scalar_tensor_tensor(SM[:], XR[:], PCT[:, Q_RK:Q_RK + 1], K2[:], ALU.mult, ALU.mult).then_inc(S("rk2"), 1)
                    dve.wait_ge(S("mm_ss"), c + 1)
                    dve.tensor_scalar(KN[:].rearrange("p (a b) -> p a b", a=2), PJ[0][:, :, 0:260], 1e-24, None, ALU.max).then_inc(S("ssm"), 1)
                    dve.wait_ge(S("mm_bo"), c + 1)
                    for b in range(2):
                        bv = dve.tensor_tensor(BV[:, 260 * b:min(260 * b + 260, T)], PJ[1][:, b, 0:min(260, T - 260 * b)],
                                               VX[:, C + 260 * b:C + min(260 * b + 260, T)], ALU.mult)
                    bv.then_inc(S("bv"), 1)
                    dve.wait_ge(S("pi"), c + 1)
                    dve.tensor_tensor(BK[:, :, 0, :], by8(K2), by8(PI), ALU.mult)
                    dve.tensor_tensor(AR[:, 1, :].rearrange("p (j t) -> p j t", j=NJ), XR[:, 0:T].rearrange("p (j t) -> p j t", j=NJ),
                                      PP[:, :, 1:C + 1], ALU.mult)
                    dve.wait_ge(S("rn"), c + 1)
                    dve.scalar_tensor_tensor(KKN[:], XK[:], PCT[:, Q_KK:Q_KK + 1], KN[:], ALU.mult, ALU.mult).then_inc(S("kkn"), 1)
                    dve.wait_ge(S("kkn"), c + 1)
                    dve.tensor_tensor(KB[:], KKN[:], AL[:], ALU.mult).then_inc(S("kb"), 1)
                    dve.tensor_tensor(AR[:, 0, :].rearrange("p (j t) -> p j t", j=NJ), KKN[:, 0:T].rearrange("p (j t) -> p j t", j=NJ),
                                      PP[:, :, 0:C], ALU.mult).then_inc(S("ar"), 1)
                    dve.wait_ge(S("kb"), c + 1)
                    dve.tensor_tensor(BK[:, :, 1, :], by8(KB), by8(PI), ALU.mult)
                    dve.tensor_tensor(BK[:, :, 2, :], by8(K2), by8(PI), ALU.mult).then_inc(S("kap"), 1)
                    if more:
                        params(c + 1)
                        for q in range(3):
                            lo(B_RKV + 3 * (c + 1) + q, rkv_slot(q))
                    for jj in range(2):
                        dve.wait_ge(S("gram"), 2 * c + jj + 1)
                        js = slice(4 * jj, 4 * jj + 4)
                        for h in range(2):
                            pr = B[2 * jj + h].rearrange("p (j t) -> p j t", j=4)
                            up, dn = HH[h], HH[1 - h]
                            m4 = lambda c0, r: CST[r, c0:c0 + C].unsqueeze(1).to_broadcast([r.stop - r.start, 4, C])
                            dve.tensor_tensor(GH[:, h, js, :], pr[:, :, C:P], m4(C_MI, slice(0, P)), ALU.mult)
                            dve.tensor_tensor(MT[up, js, :], pr[up, :, 0:C], m4(C_MN, up), ALU.mult)
                            g = dve.tensor_tensor(AN[dn, h, js, :], pr[dn, :, 0:C], m4(C_MS, dn), ALU.mult)
                        g.then_inc(S("gram_ev"), 1)
                    dve.wait_ge(S("t_v"), c + 1)
                    dve.tensor_copy(Z[0:64, 1, :, :], B[1][0:64, :].rearrange("p (j t) -> p j t", j=NJ))
                    dve.tensor_copy(SV[0:64, 1, 0:NJ, :], B[1][0:64, :].rearrange("p (j t) -> p j t", j=NJ)).then_inc(S("v_ev"), 1)
                    dve.wait_ge(S("t_bk"), c + 1)
                    dve.tensor_copy(BT[:, 1, :, :], B[3].rearrange("p (j t) -> p j t", j=NJ)).then_inc(S("bt_ev"), 1)
                    for lv in range(LEVELS):
                        dve.wait_ge(S("mm_x"), LEVELS * c + lv + 1)
                        out = TI if lv == 0 else XI
                        for h in range(2):
                            x = dve.tensor_tensor(out[HH[h]], B[h][HH[h]].rearrange("p (j t) -> p j t", j=NJ),
                                                  I2[HH[h]].unsqueeze(1).to_broadcast([HD, NJ, C]), ALU.add)
                        if lv == 0:
                            x.then_inc(S("ti_1"), 1)
                            continue
                        x.then_inc(S("xi"), 1)
                        dve.wait_ge(S("mm_tt"), (LEVELS - 1) * c + lv)
                        dve.tensor_copy(TT[HH[1]], B[3][HH[1]].rearrange("p (j t) -> p j t", j=NJ)).then_inc(S("tt1"), 1)
                        if lv == LEVELS - 1 and more:
                            dve.wait_ge(S("smp"), c + 1)
                            shift_add(B_RKV + 3 * (c + 1), XR).then_inc(S("xs"), 1)
                    for j in range(NJ):
                        dve.wait_ge(S("mm_r"), NJ * c + j + 1)
                        dve.tensor_copy(RS1[:], B[0][:, 0:C]).then_inc(S("r"), 1)
                        dve.wait_ge(S("mm_u"), NJ * c + j + 1)
                        dve.tensor_scalar(Z[HH[0], 0, j, :], B[0][HH[0], 2 * C:3 * C], -1.0, None, ALU.mult).then_inc(S("u0"), 1)
                        dve.wait_ge(S("mm_s"), NJ * c + j + 1)
                        for h in range(2):
                            s = dve.scalar_tensor_tensor(SV[HH[h], h, j + 1, :], SV[HH[h], h, j, :], PP[HH[h], j, C:C + 1],
                                                         B[0][HH[h], C:2 * C], ALU.mult, ALU.add)
                        s.then_inc(S("s"), 1)
                        if j == 3 and more:
                            shift_add(B_RKV + 3 * (c + 1) + 1, XK).then_inc(S("xs"), 1)
                    dve.wait_ge(S("mm_y"), c + 1)
                    dve.tensor_copy(YF[HH[1], :], B[3][HH[1], :]).then_inc(S("yf"), 1)
                    if more:
                        shift_add(B_RKV + 3 * (c + 1) + 2, VX[:, C:C + TN]).then_inc(S("xs"), 1)
                    dve.wait_ge(S("mm_mu"), c + 1)
                    dve.scalar_tensor_tensor(YF[:].rearrange("p (a b) -> p a b", a=2), PJ[1][:, :, 0:256], -1.0 / HD,
                                             YF[:].rearrange("p (a b) -> p a b", a=2), ALU.mult, ALU.add).then_inc(S("yc"), 1)
                    dve.wait_ge(S("grs"), c + 1)
                    dve.tensor_tensor(YF[:], YF[:], YQ[:], ALU.mult).then_inc(S("y_chain"), 1)
                    dve.wait_ge(S("y_chain"), 3 * c + 1)
                    dve.tensor_scalar(YF[:], YF[:], PCT[:, Q_GW:Q_GW + 1], PCT[:, Q_GB:Q_GB + 1], ALU.mult, ALU.add).then_inc(S("y_chain"), 1)
                    dve.wait_ge(S("y_chain"), 3 * c + 2)
                    dve.tensor_tensor(YF[:], YF[:], BV[:], ALU.add).then_inc(S("y_chain"), 1)
                    dve.wait_ge(S("y_chain"), 3 * c + 3)
                    dve.tensor_tensor(YG[:, bass.ds(c, 1), 0:T].rearrange("p a b -> p (a b)"), YF[:], G[:, 0:T], ALU.mult)
                    if more:
                        adopt(c + 1)

                dve.memset(A2[:, 0:1], 0.0)
                dve.memset(VX[:, 0:C], 0.0)
                dve.memset(PP[:, :, 0:1], 1.0)
                for h in range(2):
                    dve.memset(SV[HH[h], h, 0, :], 0.0)
                dve.tensor_scalar(OM[:, 3:5], PV[:, 0, R_ML:R_ML + 2], -1.0, 1.0, ALU.mult, ALU.add).then_inc(S("om_l"), 1)
                params(0)
                for n in range(2):
                    lo(n, n)
                shift_add(0, SW).then_inc(S("xs"), 1)
                dve.wait_ge(S("xs"), 1)
                dve.tensor_copy(TWA[64:P, :], SW[64:P, :]).then_inc(S("xl"), 1)
                lo(2, 2)
                shift_add(1, AL).then_inc(S("xs"), 1)
                dve.wait_ge(S("xs"), 2)
                dve.memset(KN[:, 0:1], 0.0).then_inc(S("xl"), 1)
                lo(3, 0)
                lo(4, 1)
                for q, x in enumerate((XR, XK, VX[:, C:C + TN])):
                    shift_add(B_RKV + q, x).then_inc(S("xs"), 1)
                dve.wait_ge(S("xs"), 5)
                adopt(0)
                tile(0, True)
                with dve.Fori(1, KT - 1) as c:
                    tile(c, True)
                tile(KT - 1, False)

            @block.gpsimd
            def _(pool):
                def tile(c):
                    at = bass.ds(c, 1)
                    flat = lambda a: a.rearrange("p a b -> p (a b)")
                    pool.wait_ge(S("ar"), c + 1)
                    settle(pool)
                    pool.tensor_copy(RHO[:], AR[:, 1, :])
                    pool.wait_ge(S("gram"), 2 * c + 2)
                    for s in range(3):
                        e = pool.tensor_tensor(BK[:, :, s, :], BK[:, :, s, :],
                                               PP[:, :, C:C + 1].to_broadcast([P, NJ, C]), ALU.mult)
                    e.then_inc(S("bke"), 1)
                    pool.wait_ge(S("kb"), c + 1)
                    pool.wait_ge(S("gte"), c + 1)
                    settle(pool)
                    for q, x in ((0, XR[:, T:TN]), (2, K2[:, T:TN]), (3, VX[:, C + T:C + TN]), (4, KKN[:, T:TN]), (5, KB[:, T:TN])):
                        pool.tensor_copy(flat(SMP[:, at, q, :]), x)
                    pool.tensor_copy(flat(GS[:, at, :]), G[:, T:TN]).then_inc(S("smp"), 1)
                    pool.wait_ge(S("gram_ev"), 2 * c + 2)
                    for lv in range(LEVELS):
                        if lv > 1:
                            pool.wait_ge(S("mm_x"), LEVELS * c + lv - 1)
                        if lv == 2:
                            pool.wait_ge(S("tt_1"), c + 1)
                        m = pool.tensor_tensor(MO[:, lv % 2], MT[:], rows8(CST[:, C_OFF + C * lv:C_OFF + C * (lv + 1)]), ALU.mult)
                        m.then_inc(S("mo"), 1)
                        if lv == 0:
                            pool.wait_ge(S("mo"), LEVELS * c + 1)
                            pool.tensor_tensor(TT[:], MO[:, 0], rows8(I2), ALU.add).then_inc(S("tt_1"), 1)

                tile(0)
                with pool.Fori(1, KT) as c:
                    tile(c)

        sb_mx = es.enter_context(ExitStack())
        MXh = sb("MXh", [P, NPOOL, TN], F32R, ctx=sb_mx)
        MXl = sb("MXl", [P, NPOOL, TN], F32R, ctx=sb_mx)
        with ExitStack() as sc:
            S0 = sb("S0", [P, HD, HD], ctx=sc)
            TA = sb("TA", [P, HD, HD], ctx=sc)
            TB = sb("TB", [P, HD, HD], ctx=sc)
            VT = sb("VT", [6 * NS, KT, P], ctx=sc)
            VEC = sb("VEC", [P, 6, HD], ctx=sc)
            RKB = sb("RKB", [P, 3, HD], ctx=sc)
            SA = sb("SA", [P, HD], ctx=sc)
            YS = sb("YS", [P, HD], ctx=sc)
            YB = sb("YB", [P, HD], ctx=sc)
            BO = sb("BO", [P, 1], ctx=sc)
            BS = sb("BS", [P, 6], ctx=sc)
            MV2 = sb("MV2", [P, 2], ctx=sc)
            YT = VT[0:NS].rearrange("b c d -> b (c d)")
            PW = sb("PW", [P, NPOOL, P], ctx=sc)
            PN = sb("PN", [P, NPOOL, PB + TC], ctx=sc)
            WS = [sb(f"WS{k}", [P, PB + T], ctx=sc) for k in range(2)]
            DF = sb("DF", [P, TN], ctx=sc)
            PS8 = sb("PS8", [P, NS], ctx=sc)
            MF = sb("MF", [P, TN], ctx=sc)
            PO = sb("PO", [PB + NS, NPOOL * P], ctx=sc)
            block = sc.enter_context(nc.Block())
            VR, VW, VK, VV, VKK, VKB = range(6)

            @block.sync
            def _(sp):
                for q in range(NPOOL):
                    w_load(sp, B_POOL + q, pool_slot(q), cols("in", 26 + q))
                sp.dma_start(S0[:].rearrange("p v k -> p (v k)"), i["state_wkv"][0].rearrange("b h v k -> (b h) (v k)")).then_inc(S("ld_s"), 16)
                for b in range(NS):
                    rows = slice(H * b, H * b + H)
                    sp.dma_start(RKB[rows, 0, :], i["r_k"][0]).then_inc(S("ld_rk"), 16)
                    sp.dma_start(RKB[rows, 1, :], i["gn_w"][0].rearrange("(h d) -> h d", h=H)).then_inc(S("ld_rk"), 16)
                    sp.dma_start(RKB[rows, 2, :], i["gn_b"][0].rearrange("(h d) -> h d", h=H)).then_inc(S("ld_rk"), 16)
                sp.dma_start(PW[:], i["pool_w"][0].rearrange("g c d -> c g d")).then_inc(S("ld_pw"), 16)
                sp.wait_ge(S("vt"), 1)
                for q in range(6):
                    sp.dma_start(VEC[:, q, :], VT[q * NS:(q + 1) * NS].rearrange("b c (h d) -> b (c h) d", h=2)).then_inc(S("ld_vec"), 16)
                sp.wait_ge(S("s_new"), 1)
                sp.dma_start(o["wkv_s"][0].rearrange("b h v k -> (b h) (v k)"), S0[:].rearrange("p v k -> p (v k)")).then_inc(S("out"), 16)
                sp.wait_ge(S("ys"), 1)
                sp.dma_start(YT[:].rearrange("b (h d) -> b h d", h=H), YS[:]).then_inc(S("ld_yt"), 16)
                sp.wait_ge(S("po"), 1)
                sp.dma_start(o["pool_p"][0, 0], PO[0:PB, :]).then_inc(S("out"), 16)
                sp.dma_start(o["pool_s"][0, :, PB - 1, :], PO[PB:PB + NS, :]).then_inc(S("out"), 16)
                for q in range(4):
                    w_load(sp, B_BR + q, q, br_src(0, q), BR_KN[q], 4 if q == 3 else 3)
                sp.wait_ge(S("out"), 16 * 7)

            def mix(pe, g):
                pe.wait_ge(S("ld_pw"), 16)
                pe.wait_ge(S("df"), g + 1)
                after(pe, "mf", g)
                for b in range(2):
                    mm = pe.matmul(B[2 + b][:, 0:260], PW[:, g, :], DF[:, 260 * b:260 * b + 260], start=True, stop=True)
                mm.then_inc(S("mm_mix"), 1)

            @block.tensor
            def _(pe):
                for c in range(KT):
                    b, r = divmod(c, 4)
                    mm = pe.transpose(B[b][0:6 * NS, r * P:(r + 1) * P], SMP[:, c].rearrange("p q b -> p (q b)"), ident)
                mm.then_inc(S("t_vt"), 1)
                for q in range(NPOOL):
                    n = B_POOL + q
                    pe.wait_ge(S("w_lo"), n + 1)
                    after(pe, "pn", q - 1)
                    for k in range(KT):
                        mm = kstep(pe, PJ[q % 2], pool_slot(q), k, Hh, Hl, k, k == 0, k == KT - 1)
                    mm.then_inc(S("prj"), 1)
                    if q > 0:
                        mix(pe, q - 1)
                mix(pe, NPOOL - 1)
                pe.wait_ge(S("vt"), 1)
                for g in range(NPOOL):
                    mm = pe.transpose(B[0][0:PB + NS, g * P:(g + 1) * P], PN[:, g, PB + T - PB:PB + TN], ident)
                mm.then_inc(S("t_po"), 1)
                pe.wait_ge(S("ld_yt"), 16)
                for c in range(KT):
                    mm = pe.transpose(B[1][:, c * NS:(c + 1) * NS], YT[:, c * P:(c + 1) * P], ident[0:NS, 0:NS])
                mm.then_inc(S("t_y"), 1)

            def mixed(act, g):
                act.wait_ge(S("mm_mix"), g + 1)
                after(act, "mxl", g)
                for b in range(2):
                    m = act.activation(MF[:, 260 * b:260 * b + 260], B[2 + b][:, 0:260], ACT.Copy, scale=PV[:, 0, R_PS + g:R_PS + g + 1])
                m.then_inc(S("mf"), 1)
                act.wait_ge(S("mf"), g + 1)
                act.activation(MXh[:, g, :], MF[:], ACT.Copy).then_inc(S("mxh"), 1)

            @block.scalar
            def _(act):
                for q in range(NPOOL):
                    n, slot = B_POOL + q, pool_slot(q)
                    act.wait_ge(S(f"w_load{slot}"), pool_loads[q])
                    act.wait_ge(S("prj"), n - 2)
                    act.activation(Wh[:, slot], RAW[:, slot], ACT.Copy).then_inc(S("w_hi"), 1)
                act.wait_ge(S("t_vt"), 1)
                for b in range(2):
                    v = act.activation(VT[:, 4 * b:4 * b + 4, :].rearrange("p c d -> p (c d)"), B[b][0:6 * NS, :], ACT.Copy)
                v.then_inc(S("vt"), 1)
                for q in range(NPOOL):
                    act.wait_ge(S("prj"), B_POOL + q + 1)
                    act.activation(PN[:, q, PB:PB + TC].rearrange("p (a b) -> p a b", a=2), PJ[q % 2][:, :, 0:HC], ACT.Copy).then_inc(S("pn"), 1)
                    if q > 0:
                        mixed(act, q - 1)
                mixed(act, NPOOL - 1)
                act.wait_ge(S("t_po"), 1)
                act.activation(PO[:], B[0][0:PB + NS, :], ACT.Copy).then_inc(S("po"), 1)
                act.wait_ge(S("mv2"), 1)
                act.activation(BO[:], MV2[:, 1:2], ACT.Sqrt, bias=CST[:, C_EPS + 1:C_EPS + 2]).then_inc(S("sd2"), 1)

            def mix_lo(dve, g):
                dve.wait_ge(S("mxh"), g + 1)
                dve.tensor_tensor(MXl[:, g, :], MF[:], MXh[:, g, :].bitcast(F32), ALU.subtract).then_inc(S("mxl"), 1)

            @block.vector
            def _(dve):
                for w in WS:
                    dve.memset(w[:, 0:PB], 0.0)
                dve.memset(PN[:, :, 0:PB], 0.0).then_inc(S("pz"), 1)
                for q in range(NPOOL):
                    n, slot = B_POOL + q, pool_slot(q)
                    dve.wait_ge(S("w_hi"), n + 1)
                    dve.tensor_tensor(Wl[:, slot], RAW[:, slot], Wh[:, slot].bitcast(F32), ALU.subtract).then_inc(S("w_lo"), 1)
                dve.wait_ge(S("pz"), 1)
                steps = 0
                for g in range(NPOOL):
                    dve.wait_ge(S("pn"), g + 1)
                    x, last = PN[:, g], 0
                    for lv in range(g + 1):
                        m, lo_ = 1 << lv, (2 << lv) - 1
                        y = WS[lv % 2]
                        dve.tensor_tensor(y[:, lo_:PB + T], x[:, lo_:PB + T], x[:, lo_ - m:PB + T - m], ALU.add).then_inc(S("ws_"), 1)
                        steps += 1
                        dve.wait_ge(S("ws_"), steps)
                        x = y
                    dve.tensor_tensor(x[:, PB:PB + 16], x[:, PB:PB + 16], CST[:, C_IC + 16 * g:C_IC + 16 * g + 16], ALU.mult).then_inc(S("ws_"), 1)
                    dve.tensor_copy(PLS[:, g, PB, :], PN[:, g, PB + T:PB + TN]).then_inc(S("ws_"), 1)
                    steps += 2
                    dve.wait_ge(S("ws_"), steps)
                    w = 2 << g
                    after(dve, "mm_mix", g)
                    dve.scalar_tensor_tensor(DF[:, 0:T], x[:, PB:PB + T], 1.0 / w, PN[:, g, PB:PB + T], ALU.mult, ALU.subtract)
                    dve.tensor_reduce(PS8[:], PLS[:, g, 16 - w:16, :].rearrange("p t b -> p b t"), AX.X, ALU.add).then_inc(S("ws_"), 1)
                    steps += 1
                    dve.wait_ge(S("ws_"), steps)
                    dve.scalar_tensor_tensor(DF[:, T:TN], PS8[:], 1.0 / w, PN[:, g, PB + T:PB + TN], ALU.mult, ALU.subtract).then_inc(S("df"), 1)
                    if g > 0:
                        mix_lo(dve, g - 1)
                mix_lo(dve, NPOOL - 1)
                kb3 = lambda q: VEC[:, q, :].unsqueeze(1).to_broadcast([P, HD, HD])
                v3 = lambda a: a.unsqueeze(2).to_broadcast([P, HD, HD])
                dve.wait_ge(S("ld_s"), 16)
                dve.wait_ge(S("ld_vec"), 96)
                dve.tensor_tensor(TA[:], S0[:], kb3(VKK), ALU.mult).then_inc(S("rs_"), 1)
                dve.wait_ge(S("rs_"), 1)
                dve.tensor_reduce(SA[:], TA[:], AX.X, ALU.add).then_inc(S("rs_"), 1)
                dve.tensor_tensor(S0[:], S0[:], kb3(VW), ALU.mult).then_inc(S("rs_"), 1)
                dve.wait_ge(S("rs_"), 3)
                dve.tensor_tensor(TA[:], v3(SA[:]), kb3(VKB), ALU.mult).then_inc(S("rs_"), 1)
                dve.wait_ge(S("rs_"), 4)
                dve.tensor_tensor(S0[:], S0[:], TA[:], ALU.subtract).then_inc(S("rs_"), 1)
                dve.wait_ge(S("rs_"), 5)
                dve.wait_ge(S("vk"), 1)
                dve.tensor_tensor(S0[:], S0[:], TB[:], ALU.add).then_inc(S("s_new"), 1)
                dve.wait_ge(S("s_new"), 1)
                dve.tensor_tensor(TA[:], S0[:], kb3(VR), ALU.mult).then_inc(S("rs_"), 1)
                dve.wait_ge(S("rs_"), 6)
                dve.tensor_reduce(YS[:], TA[:], AX.X, ALU.add).then_inc(S("rs_"), 1)
                dve.wait_ge(S("rs_"), 7)
                dve.bn_stats(BS[:], YS[:]).then_inc(S("rs_"), 1)
                dve.wait_ge(S("rs_"), 8)
                dve.bn_aggr(MV2[:], BS[:]).then_inc(S("mv2"), 1)
                dve.wait_ge(S("ld_rk"), 16 * 24)
                dve.wait_ge(S("mv2"), 1)
                dve.tensor_tensor(SA[:], VEC[:, VR, :], VEC[:, VK, :], ALU.mult).then_inc(S("rs_"), 1)
                dve.wait_ge(S("rs_"), 9)
                dve.tensor_tensor(YB[:], SA[:], RKB[:, 0, :], ALU.mult).then_inc(S("rs_"), 1)
                dve.wait_ge(S("rs_"), 10)
                dve.tensor_reduce(BS[:, 0:1], YB[:], AX.X, ALU.add).then_inc(S("rs_"), 1)
                dve.wait_ge(S("sd2"), 1)
                dve.reciprocal(BO[:], BO[:]).then_inc(S("rs_"), 1)
                dve.wait_ge(S("rs_"), 12)
                dve.tensor_scalar(YS[:], YS[:], MV2[:, 0:1], BO[:], ALU.subtract, ALU.mult).then_inc(S("rs_"), 1)
                dve.wait_ge(S("rs_"), 13)
                dve.tensor_tensor(YS[:], YS[:], RKB[:, 1, :], ALU.mult).then_inc(S("rs_"), 1)
                dve.wait_ge(S("rs_"), 14)
                dve.tensor_tensor(YS[:], YS[:], RKB[:, 2, :], ALU.add).then_inc(S("rs_"), 1)
                dve.wait_ge(S("rs_"), 15)
                dve.scalar_tensor_tensor(YS[:], VEC[:, VV, :], BS[:, 0:1], YS[:], ALU.mult, ALU.add).then_inc(S("ys"), 1)
                dve.wait_ge(S("t_y"), 1)
                dve.tensor_tensor(YG[:, :, T:TN], B[1][:, 0:KT * NS].rearrange("p (c b) -> p c b", c=KT), GS[:], ALU.mult)

            @block.gpsimd
            def _(pool):
                pool.wait_ge(S("ld_vec"), 96)
                pool.tensor_tensor(TB[:], VEC[:, VV, :].unsqueeze(2).to_broadcast([P, HD, HD]),
                                   VEC[:, VK, :].unsqueeze(1).to_broadcast([P, HD, HD]), ALU.mult).then_inc(S("vk"), 1)

        with ExitStack() as sc:
            YGh = sb("YGh", [P, KT, TN], F32R, ctx=sc)
            YGl = sb("YGl", [P, KT, TN], F32R, ctx=sc)
            MGh = sb("MGh", [P, KT, TN], F32R, ctx=sc)
            MGl = sb("MGl", [P, KT, TN], F32R, ctx=sc)
            SGP = sb("SGP", [P, TN], ctx=sc)
            SGR = sb("SGR", [P, TN], ctx=sc)
            M1 = sb("M1", [P, TN], ctx=sc)
            M2 = sb("M2", [P, TN], ctx=sc)
            block = sc.enter_context(nc.Block())
            two = lambda a: a.rearrange("p (a b) -> p a b", a=2)
            nb = (260, 260)
            dyn = lambda a, e: a[:, bass.ds(e, 1), :].rearrange("p a b -> p (a b)")

            @block.sync
            def _(sp):
                with sp.Fori(1, KT) as e:
                    for q in range(4):
                        w_load(sp, B_BR + 4 * e + q, q, br_src(e, q), BR_KN[q], 4)
                for e in range(KT):
                    w_load(sp, B_OUT + e, e % 4, cols("out", e), ring=4)
                for q in range(4):
                    w_load(sp, B_FF + q, q, ff_src(0, q), ring=4)

            @block.tensor
            def _(pe):
                def tile(e):
                    for q, (x, pj) in enumerate((((Hh, Hl), 0), ((Hh, Hl), 1), ((YGh, YGl), 0), ((MXh, MXl), 1))):
                        pe.wait_ge(S("w_lo"), B_BR + 4 * e + q + 1)
                        if q < 2:
                            after(pe, ("m_r", "m_p")[q], e)
                        else:
                            pe.wait_ge(S(("sg_p", "sg_r")[q - 2]), e + 1)
                        if q == 2 and isinstance(e, int):
                            pe.wait_ge(S("ygl"), KT)
                        for k in range(BR_KN[q]):
                            mm = kstep(pe, PJ[pj], q, k, x[0], x[1], k, k == 0, k == BR_KN[q] - 1, nb)
                        mm.then_inc(S("prj"), 1)

                tile(0)
                with pe.Fori(1, KT) as e:
                    tile(e)
                pe.wait_ge(S("mgl"), KT)
                for e in range(KT):
                    pe.wait_ge(S("w_lo"), B_OUT + e + 1)
                    after(pe, "mo1_s", e - 1)
                    if e < 2:
                        pe.wait_ge(S(("m_r", "m_p")[e]), KT)
                    for k in range(KT):
                        mm = kstep(pe, PJ[e % 2], e % 4, k, MGh, MGl, k, k == 0, k == KT - 1, nb)
                    mm.then_inc(S("prj"), 1)

            def gated(act, e):
                act.wait_ge(S("prj"), B_OUT + e + 1)
                act.activation(MO1[:, e, 0:260], PJ[e % 2][:, 0, 0:260], ACT.Copy, scale=MOD[:, 2 * KT + e, 0:1])
                act.activation(MO1[:, e, 260:T], PJ[e % 2][:, 1, 0:T - 260], ACT.Copy, scale=MOD[:, 2 * KT + e, 0:1]).then_inc(S("mo1"), 1)

            @block.scalar
            def _(act):
                def split(n, slot, loads, kn=KT):
                    act.wait_ge(S(f"w_load{slot}"), loads)
                    act.wait_ge(S("prj"), n - 2)
                    act.activation(Wh[:, slot, 0:kn], RAW[:, slot, 0:kn], ACT.Copy).then_inc(S("w_hi"), 1)

                def tile(e):
                    for q in range(2, 4):
                        split(B_BR + 4 * e + q, q, br_loads[q] + 16 * e, BR_KN[q])
                        if q == 2:
                            act.wait_ge(S("prj"), B_BR + 4 * e + 1)
                            after(act, "m_p", e)
                            act.activation(two(SGP[:]), PJ[0][:, :, 0:260], ACT.Sigmoid).then_inc(S("sg_p"), 1)
                    act.wait_ge(S("prj"), B_BR + 4 * e + 2)
                    act.activation(two(SGR[:]), PJ[1][:, :, 0:260], ACT.Sigmoid).then_inc(S("sg_r"), 1)
                    for q in range(2):
                        split(B_BR + 4 * (e + 1) + q, q, br_loads[q] + 16 * (e + 1))
                    act.wait_ge(S("mg"), e + 1)
                    act.activation(dyn(MGh, e), M1[:], ACT.Copy).then_inc(S("mgh"), 1)

                for c in range(KT):
                    act.activation(YGh[:, c, :], YG[:, c, :], ACT.Copy).then_inc(S("ygh"), 1)
                for q in range(2):
                    split(B_BR + q, q, br_loads[q])
                tile(0)
                with act.Fori(1, KT) as e:
                    tile(e)
                for e in range(KT):
                    if e > 1:
                        split(B_OUT + e, e % 4, br_loads[e % 4] + 16 * KT + 16 * (e // 4))
                    if e > 0:
                        gated(act, e - 1)
                gated(act, KT - 1)

            def gated_s(dve, e):
                dve.wait_ge(S("mo1"), e + 1)
                dve.tensor_tensor(MO1[:, e, T:TN], PJ[e % 2][:, 1, T - 260:260], MOD[:, 2 * KT + e, 1:NMOD], ALU.mult).then_inc(S("mo1_s"), 1)
            @block.vector
            def _(dve):
                def lo(n, slot, kn=KT):
                    dve.wait_ge(S("w_hi"), n + 1)
                    dve.tensor_tensor(Wl[:, slot, 0:kn], RAW[:, slot, 0:kn], Wh[:, slot, 0:kn].bitcast(F32), ALU.subtract).then_inc(S("w_lo"), 1)

                def tile(e):
                    for q in range(2, 4):
                        lo(B_BR + 4 * e + q, q, BR_KN[q])
                    for q in range(2):
                        lo(B_BR + 4 * (e + 1) + q, q)
                    dve.wait_ge(S("sg_r"), e + 1)
                    after(dve, "mgh", e)
                    dve.wait_ge(S("prj"), B_BR + 4 * e + 3)
                    dve.tensor_tensor(two(M1[:]), PJ[0][:, :, 0:260], two(SGR[:]), ALU.mult).then_inc(S("m_r"), 1)
                    dve.wait_ge(S("prj"), B_BR + 4 * e + 4)
                    dve.tensor_tensor(two(M2[:]), PJ[1][:, :, 0:260], two(SGP[:]), ALU.mult).then_inc(S("m_p"), 1)
                    dve.wait_ge(S("m_p"), e + 1)
                    dve.tensor_tensor(M1[:], M1[:], M2[:], ALU.add).then_inc(S("mg"), 1)
                    dve.wait_ge(S("mgh"), e + 1)
                    dve.tensor_tensor(dyn(MGl, e), M1[:], dyn(MGh, e).bitcast(F32), ALU.subtract).then_inc(S("mgl"), 1)

                for q in range(2):
                    lo(B_BR + q, q)
                for c in range(KT):
                    dve.wait_ge(S("ygh"), c + 1)
                    dve.tensor_tensor(YGl[:, c, :], YG[:, c, :], YGh[:, c, :].bitcast(F32), ALU.subtract).then_inc(S("ygl"), 1)
                tile(0)
                with dve.Fori(1, KT) as e:
                    tile(e)
                for e in range(KT):
                    if e > 1:
                        lo(B_OUT + e, e % 4)
                    if e > 0:
                        gated_s(dve, e - 1)
                gated_s(dve, KT - 1)

        sb_mx.close()

        def residual_norm(stage, xsrc, delta, lnw, lnb, tail):
            s = S
            done = {"hf": KT + 1, "hh": KT, "xn": 5, "mv": 5, "sd": 1, "chain": 9, "t_x": KT, "t_s": 1}
            if tail == "y":
                done = {"ld": 64, "x1": 5, "st": 80, "td": 5, "sd": 11, "mv": 15, "chain": 9 + 5 * 7 + 1}

            def wait(eng, name, n):
                eng.wait_ge(s(name), done.get(name, 0) + n)

            def behind(eng, name, n):
                if n > 0:
                    wait(eng, name, n)

            with ExitStack() as sc:
                XA = sb(f"XA{stage}", [P, 5, D], ctx=sc)
                LNP = sb(f"LNP{stage}", [P, 2, D], ctx=sc)
                ST = sb(f"ST{stage}", [P, 2, 6], ctx=sc)
                MV_ = sb(f"MV{stage}", [P, 2], ctx=sc)
                SD_ = sb(f"SD{stage}", [P, 1], ctx=sc)
                RS_ = sb(f"RS{stage}", [P, 1], ctx=sc)
                XN_ = sb(f"XN{stage}", [P, 5, D], ctx=sc) if tail == "h2" else None
                HF = sb(f"HF{stage}", [P, KT, TN], ctx=sc) if tail == "h2" else None
                CO = sb(f"CO{stage}", [2 + NS, 2 * FF], ctx=sc) if tail == "y" else None
                block = sc.enter_context(nc.Block())
                rows = [P] * 4 + [NS]

                @block.sync
                def _(sp):
                    if tail == "h2":
                        sp.dma_start(XA[:, 0:4, :], xsrc[0][0].rearrange("(a p) d -> p a d", p=P)).then_inc(s("ld"), 16)
                        sp.dma_start(XA[0:NS, 4, :], xsrc[1][:, 0, :]).then_inc(s("ld"), 16)
                    else:
                        sp.dma_start(XA[:, 0:4, :], xsrc[0].rearrange("(a p) d -> p a d", p=P)).then_inc(s("ld"), 16)
                        sp.dma_start(XA[0:NS, 4, :], xsrc[1]).then_inc(s("ld"), 16)
                    for k, v in enumerate((lnw, lnb)):
                        sp.dma_start(LNP[:, k, :], i[v].to_broadcast([P, D])).then_inc(s("ld"), 16)
                    for t in range(5):
                        wait(sp, "x1", t + 1)
                        n = rows[t]
                        if tail == "h2":
                            dst = X1D[t * P:t * P + n, :]
                        else:
                            dst = o["y_p"][0, t * P:(t + 1) * P, :] if t < 4 else o["y_s"][:, 0, :]
                        sp.dma_start(dst, XA[0:n, t, :]).then_inc(s("st"), 16)
                    if tail == "y":
                        wait(sp, "co", 2 * FT // 4)
                        sp.dma_start(o["conv_p"][0, 0], CO[0:2, :]).then_inc(s("st"), 16)
                        sp.dma_start(o["conv_s"][0, :, 1, :], CO[2:2 + NS, :]).then_inc(s("st"), 16)
                    wait(sp, "st", 16 * (5 if tail == "h2" else 7))

                @block.tensor
                def _(pe):
                    for t in range(5):
                        n = rows[t]
                        behind(pe, "x1", t - 1)
                        for k in range(KT):
                            b, r = divmod(k, 4)
                            mm = pe.transpose(PJ[t % 2][0:n, b, r * P:(r + 1) * P], delta[:, k, t * P:t * P + n], ident)
                        mm.then_inc(s("td"), 1)
                    if tail == "h2":
                        for t in range(4):
                            wait(pe, "xn", t + 1)
                        for k in range(KT):
                            behind(pe, "hf", k - 1)
                            for t in range(4):
                                mm = pe.transpose(B[k % 2][:, t * P:(t + 1) * P], XN_[:, t, k * P:(k + 1) * P], ident)
                            mm.then_inc(s("t_x"), 1)
                        wait(pe, "xn", 5)
                        for k in range(KT):
                            mm = pe.transpose(B[2][:, k * NS:(k + 1) * NS], XN_[0:NS, 4, k * P:(k + 1) * P], ident[0:NS, 0:NS])
                        mm.then_inc(s("t_s"), 1)
                    else:
                        for f in range(2 * FT):
                            g, r = divmod(f, 4)
                            if r == 0:
                                behind(pe, "co", g - 1)
                            mm = pe.transpose(B[g % 2][0:2 + NS, r * P:(r + 1) * P], UO[:, f, :], ident)
                            if r == 3:
                                mm.then_inc(s("tc"), 1)

                @block.scalar
                def _(act):
                    for t in range(5):
                        n = rows[t]
                        for r in range(2 if tail == "h2" else 1):
                            wait(act, "mv", (2 if tail == "h2" else 1) * t + r + 1)
                            act.activation(SD_[0:n, :], MV_[0:n, 1:2], ACT.Sqrt, bias=CST[0:n, C_EPS:C_EPS + 1]).then_inc(s("sd"), 1)
                    if tail == "h2":
                        for k in range(KT):
                            wait(act, "t_x", k + 1)
                            act.activation(HF[:, k, 0:T], B[k % 2][:], ACT.Identity, bias=MOD[:, 3 * KT + k, 0:1],
                                           scale=MOD[:, 4 * KT + k, 0:1]).then_inc(s("hf"), 1)
                        for k in range(KT):
                            wait(act, "hf", KT + 1)
                            act.activation(Hh[:, k, 0:TN], HF[:, k, :], ACT.Copy).then_inc(s("hh"), 1)
                    else:
                        for g in range(2 * FT // 4):
                            wait(act, "tc", g + 1)
                            act.activation(CO[:, g * 512:(g + 1) * 512], B[g % 2][0:2 + NS, :], ACT.Copy).then_inc(s("co"), 1)

                @block.vector
                def _(dve):
                    cnt = {"mv": 0, "c": 0}

                    def chain(ins):
                        cnt["c"] += 1
                        ins.then_inc(s("chain"), 1)
                        wait(dve, "chain", cnt["c"])

                    def norm(out, x, n):
                        for b in range(2):
                            bs = dve.bn_stats(ST[0:n, b, :], x[:, b * 512:(b + 1) * 512])
                        chain(bs)
                        cnt["mv"] += 1
                        dve.bn_aggr(MV_[0:n, :], ST[0:n].rearrange("p a b -> p (a b)")).then_inc(s("mv"), 1)
                        wait(dve, "sd", cnt["mv"])
                        chain(dve.reciprocal(RS_[0:n, :], SD_[0:n, :]))
                        return dve.tensor_scalar(out, x, MV_[0:n, 0:1], RS_[0:n, :], ALU.subtract, ALU.mult)

                    wait(dve, "ld", 64)
                    for t in range(5):
                        n = rows[t]
                        x = XA[0:n, t, :]
                        wait(dve, "td", t + 1)
                        chain(dve.scalar_tensor_tensor(x.rearrange("p (a b) -> p a b", a=2), x.rearrange("p (a b) -> p a b", a=2), ALPHA,
                                                       PJ[t % 2][0:n, :, :], ALU.mult, ALU.add))
                        chain(norm(x, x, n))
                        chain(dve.tensor_tensor(x, x, LNP[0:n, 0, :], ALU.mult))
                        dve.tensor_tensor(x, x, LNP[0:n, 1, :], ALU.add).then_inc(s("x1"), 1)
                        wait(dve, "x1", t + 1)
                        if tail == "h2":
                            norm(XN_[0:n, t, :], x, n).then_inc(s("xn"), 1)
                            wait(dve, "xn", t + 1)
                    if tail == "h2":
                        wait(dve, "t_s", 1)
                        chain(dve.tensor_tensor(HF[:, :, T:TN], B[2][:, 0:KT * NS].rearrange("p (a b) -> p a b", a=KT),
                                                MOD[:, 4 * KT:5 * KT, 1:NMOD], ALU.mult))
                        dve.tensor_tensor(HF[:, :, T:TN], HF[:, :, T:TN], MOD[:, 3 * KT:4 * KT, 1:NMOD], ALU.add).then_inc(s("hf"), 1)
                        for k in range(KT):
                            wait(dve, "hh", k + 1)
                            dve.tensor_tensor(Hl[:, k, 0:TN], HF[:, k, :], Hh[:, k, 0:TN].bitcast(F32), ALU.subtract)

        X1D = nc.dram_tensor("x1_rows", (TN, D), F32, kind="Internal").ap()
        residual_norm("_1", (i["x_prompt"], i["x_sample"]), MO1, "ln1_w", "ln1_b", "h2")

        with ExitStack() as sc:
            SFh = sb("SFh", [P, FT, TN], F32R, ctx=sc)
            SFl = sb("SFl", [P, FT, TN], F32R, ctx=sc)
            SG = sb("SG", [P, TN], ctx=sc)
            CP = sb("CP", [P, 4, 2, 2], ctx=sc)
            block = sc.enter_context(nc.Block())
            two = lambda a: a.rearrange("p (a b) -> p a b", a=2)
            nb = (260, 260)
            PQ = [PJ[0], PJ[1], BB[:, 0:2, :], BB[:, 2:4, :]]
            dyn = lambda a, e: a[:, bass.ds(e, 1), :].rearrange("p a b -> p (a b)")
            NM = FT // 2

            @block.sync
            def _(sp):
                with sp.Fori(1, NM) as m:
                    for q in range(4):
                        w_load(sp, B_FF + 4 * m + q, q, ff_src(m, q), ring=4)
                for q in range(3):
                    w_load(sp, B_DN + q, q, dn_src(0, q), DN_KN[q], 4)
                with sp.Fori(1, KT) as e:
                    for q in range(3):
                        w_load(sp, B_DN + 3 * e + q, q, dn_src(e, q), DN_KN[q])

            @block.tensor
            def _(pe):
                def pair(m):
                    for q in range(4):
                        pe.wait_ge(S("w_lo"), B_FF + 4 * m + q + 1)
                        after(pe, "u_ev", 4 * m + q - 3)
                        for k in range(KT):
                            mm = kstep(pe, PQ[q], q, k, Hh, Hl, k, k == 0, k == KT - 1, nb)
                        mm.then_inc(S("prj"), 1)

                pair(0)
                with pe.Fori(1, NM) as m:
                    pair(m)
                pe.wait_ge(S("sfl"), FT)
                pe.wait_ge(S("u_ev"), 4 * NM)

                def down(e2):
                    for r in range(2):
                        after(pe, "fd_2", 2 * e2 + r - 1)
                        for q in range(3):
                            pe.wait_ge(S("w_lo"), B_DN + 6 * e2 + 3 * r + q + 1)
                            for k in range(DN_KN[q]):
                                mm = kstep(pe, PJ[r], q, k, SFh, SFl, 8 * q + k, q == 0 and k == 0, q == 2 and k == DN_KN[2] - 1, nb)
                            mm.then_inc(S("prj"), 1)

                down(0)
                with pe.Fori(1, KT // 2) as e2:
                    down(e2)

            @block.scalar
            def _(act):
                def split(n, slot, loads, kn=KT):
                    act.wait_ge(S(f"w_load{slot}"), loads)
                    act.wait_ge(S("prj"), n - 2)
                    act.activation(Wh[:, slot, 0:kn], RAW[:, slot, 0:kn], ACT.Copy).then_inc(S("w_hi"), 1)

                def tile(m, r, more):
                    act.wait_ge(S("cp"), m + 1)
                    for hf in range(2):
                        q = 2 * r + hf
                        act.wait_ge(S("prj"), B_FF + 4 * m + q + 1)
                        after(act, "uo", 2 * m + r - 1)
                        after(act, "sfl", 2 * m + r - 1)
                        act.activation(two(U[r][hf][:, 2:2 + TN]), PQ[q][:, :, 0:260], ACT.Copy)
                        act.activation(two(CV[r][hf]), PQ[q][:, :, 0:260], ACT.Identity, bias=CP[:, 3, hf, r:r + 1],
                                       scale=CP[:, 2, hf, r:r + 1]).then_inc(S("u_ev"), 1)
                        if more:
                            split(B_FF + 4 * (m + 1) + q, q, ff_loads[q] + 16 * (m + 1))
                    act.wait_ge(S("cv"), 4 * (2 * m + r) + 2)
                    act.activation(SG[:], CV[r][1], ACT.Sigmoid).then_inc(S("sg"), 1)
                    act.wait_ge(S("sf"), 2 * m + r + 1)
                    act.activation(dyn(SFh, 2 * m + r), CV[r][0], ACT.Copy).then_inc(S("sfh"), 1)

                for q in range(4):
                    split(B_FF + q, q, ff_loads[q])
                for r in range(2):
                    tile(0, r, True)
                with act.Fori(1, NM - 1) as m:
                    for r in range(2):
                        tile(m, r, True)
                for r in range(2):
                    tile(NM - 1, r, False)
                act.wait_ge(S("uo"), FT)
                act.wait_ge(S("sfl"), FT)

                def down(e2, first, last):
                    for r in range(2):
                        e = 2 * e2 + r
                        for q in range(3):
                            split(B_DN + 3 * e + q, q, ff_loads[q] + 16 * (NM + e), DN_KN[q])
                        if r == 1 or not first:
                            down_out(e - 1, 1 - r)
                    if last:
                        down_out(e, 1)

                def down_out(e, r):
                    act.wait_ge(S("prj"), B_DN + 3 * e + 3)
                    act.wait_ge(S("g2"), e + 1)
                    row = FD[:, bass.ds(e, 1), :].rearrange("p a b -> p (a b)")
                    act.activation(row[:, 0:260], PJ[r][:, 0, 0:260], ACT.Copy, scale=G2[:, r, 0:1])
                    act.activation(row[:, 260:T], PJ[r][:, 1, 0:T - 260], ACT.Copy, scale=G2[:, r, 0:1]).then_inc(S("fd_1"), 1)

                down(0, True, False)
                with act.Fori(1, KT // 2 - 1) as e2:
                    down(e2, False, False)
                down(KT // 2 - 1, False, True)

            @block.vector
            def _(dve):
                def lo(n, slot, kn=KT):
                    dve.wait_ge(S("w_hi"), n + 1)
                    dve.tensor_tensor(Wl[:, slot, 0:kn], RAW[:, slot, 0:kn], Wh[:, slot, 0:kn].bitcast(F32), ALU.subtract).then_inc(S("w_lo"), 1)

                def params(m):
                    after(dve, "u_ev", 4 * m)
                    halves = lambda a: a.rearrange("p (h f) -> p h f", h=2)[:, :, bass.ds(2 * m, 2)]
                    dve.tensor_copy(CP[:, 0], halves(PV[:, 2, 0:44]))
                    dve.tensor_copy(CP[:, 1], halves(PV[:, 2, 44:88]))
                    dve.tensor_copy(CP[:, 2], halves(PV[:, 3, 0:44]))
                    dve.tensor_copy(CP[:, 3], halves(PV[:, 1, ADA:ADA + 44])).then_inc(S("cp"), 1)

                def tile(m, r, more):
                    dve.wait_ge(S("cp"), m + 1)
                    for hf in (1, 0):
                        dve.wait_ge(S("u_ev"), 4 * m + 2 * r + 2)
                        cv, u = CV[r][hf], U[r][hf]
                        st = SCV[:, bass.ds(2 * m + r + FT * hf, 1)].rearrange("p a b t -> p (a b) t")
                        base = (2 * m + r) * 4 + 2 * (1 - hf)
                        for k in (1, 0):
                            w = CP[:, k, hf, r:r + 1]
                            dve.scalar_tensor_tensor(cv[:, 0:T], u[:, k:k + T], w, cv[:, 0:T], ALU.mult, ALU.add)
                            dve.scalar_tensor_tensor(cv[:, T:TN], st[:, :, k], w, cv[:, T:TN], ALU.mult, ALU.add).then_inc(S("cv"), 1)
                            dve.wait_ge(S("cv"), base + (1 - k) + 1)
                        if more:
                            lo(B_FF + 4 * (m + 1) + 2 * r + (1 - hf), 2 * r + (1 - hf))
                    dve.wait_ge(S("sg"), 2 * m + r + 1)
                    dve.tensor_tensor(CV[r][1], CV[r][1], SG[:], ALU.mult).then_inc(S("silu"), 1)
                    dve.wait_ge(S("silu"), 2 * m + r + 1)
                    dve.tensor_tensor(CV[r][0], CV[r][0], CV[r][1], ALU.mult).then_inc(S("sf"), 1)
                    dve.wait_ge(S("sfh"), 2 * m + r + 1)
                    dve.tensor_tensor(dyn(SFl, 2 * m + r), CV[r][0], dyn(SFh, 2 * m + r).bitcast(F32), ALU.subtract).then_inc(S("sfl"), 1)

                for r in range(2):
                    for u in U[r]:
                        z = dve.memset(u[:, 0:2], 0.0)
                params(0)
                for q in range(4):
                    lo(B_FF + q, q)
                for r in range(2):
                    tile(0, r, True)
                with dve.Fori(1, NM - 1) as m:
                    params(m)
                    for r in range(2):
                        tile(m, r, True)
                params(NM - 1)
                for r in range(2):
                    tile(NM - 1, r, False)
                def down(e2, first, last):
                    for r in range(2):
                        e = 2 * e2 + r
                        for q in range(3):
                            lo(B_DN + 3 * e + q, q, DN_KN[q])
                        if r == 1 or not first:
                            down_out(e - 1, 1 - r)
                        gate(e, r)
                    if last:
                        down_out(e, 1)

                def gate(e, r):
                    after(dve, "fd_2", e - 1)
                    dve.tensor_copy(G2[:, r:r + 1, :], MOD[:, bass.ds(e + 5 * KT, 1), :]).then_inc(S("g2"), 1)

                def down_out(e, r):
                    dve.wait_ge(S("fd_1"), e + 1)
                    dve.tensor_tensor(FD[:, bass.ds(e, 1), T:TN].rearrange("p a b -> p (a b)"), PJ[r][:, 1, T - 260:260],
                                      G2[:, r, 1:NMOD], ALU.mult).then_inc(S("fd_2"), 1)

                dve.wait_ge(S("uo"), FT)
                down(0, True, False)
                with dve.Fori(1, KT // 2 - 1) as e2:
                    down(e2, False, False)
                down(KT // 2 - 1, False, True)

            @block.gpsimd
            def _(pool):
                def tile(m, r):
                    pool.wait_ge(S("u_ev"), 4 * m + 2 * r + 2)
                    pool.wait_ge(S("sf"), 2 * m + r + 1)
                    settle(pool)
                    for hf in range(2):
                        u = pool.tensor_copy(UO[:, bass.ds(2 * m + r + FT * hf, 1), :].rearrange("p a b -> p (a b)"), U[r][hf][:, T:2 + TN])
                    u.then_inc(S("uo"), 1)

                with pool.Fori(0, NM) as m:
                    for r in range(2):
                        tile(m, r)

        residual_norm("_2", (X1D[0:T, :], X1D[T:TN, :]), FD, "ln2_w", "ln2_b", "y")


NAMES = ['x_prompt', 'x_sample', 'state_shift', 'state_wkv', 'state_pool', 'state_conv', 'c_prompt', 'c_sample',
         'ada_w', 'ada_b', 'w_in', 'mu_shift', 'decay_w0', 'decay_up', 'aaa_a0', 'aaa_up', 'gate_up', 'k_k', 'k_a', 'r_k',
         'gn_w', 'gn_b', 'w_branch_rwkv', 'pool_w', 'pool_scale', 'w_branch_pool', 'w_out', 'ln1_w', 'ln1_b',
         'ffn_up', 'conv_w', 'conv_b', 'ffn_down', 'ln2_w', 'ln2_b']
OUTS = {
    'y_p': (1, T, D), 'y_s': (NS, 1, D), 'shift_p': (1, 1, D), 'wkv_p': (1, 1, H, HD, HD), 'pool_p': (1, 1, PB, NPOOL * P),
    'conv_p': (1, 1, 2, 2 * FF), 'shift_s': (1, NS, D), 'wkv_s': (1, NS, H, HD, HD), 'pool_s': (1, NS, PB, NPOOL * P),
    'conv_s': (1, NS, 2, 2 * FF),
}


def kernel(**inputs):
    import numpy as _np
    import concourse.bacc as _bacc
    from concourse import mybir as _mybir
    from concourse.bass_utils import run_bass_kernel_spmd as _run

    nc = _bacc.Bacc("TRN2", target_bir_lowering=False, num_devices=1)
    arrays, ins, outs = {}, {}, {}
    for name in NAMES + ['consts']:
        a = shape_constants() if name == 'consts' else _np.ascontiguousarray(inputs[name])
        arrays[f"in_{name}_dram"] = a
        ins[name] = nc.dram_tensor(f"in_{name}_dram", a.shape, _mybir.dt.from_np(a.dtype), kind="ExternalInput").ap()
    for name, shape in OUTS.items():
        outs[name] = nc.dram_tensor(f"out_{name}_dram", shape, F32, kind="ExternalOutput").ap()
    build(nc, ins, outs)
    r = _run(nc, [arrays], core_ids=[0])
    return tuple(r.results[0][f"out_{name}_dram"] for name in OUTS)
```
